# Optimizing a Trainium2 kernel written in Bass

```python
import jax
import jax.numpy as jnp
from jax import lax
import numpy as np

D_MODEL = 1024
BATCH = 1
SEQ = 512
DEPTH = 2

CHUNK = 64
D_FF = 2816
D_CONV = 512
CONV_WIDTH = 31
GLA_HEADS = 4
GLA_DK = 64
GLA_DV = 128
D_GLA = GLA_HEADS * GLA_DV
D_MIX = D_CONV + D_GLA
GATE_RANK = 16
GATE_TAU = 16.0
N_MOD = 9
EPS = 1e-6
SPLITS = (D_CONV, 2 * D_CONV, 2 * D_CONV + GLA_HEADS * GLA_DK, 2 * D_CONV + 2 * GLA_HEADS * GLA_DK, 2 * D_CONV + 2 * GLA_HEADS * GLA_DK + D_GLA, 2 * D_CONV + 2 * GLA_HEADS * GLA_DK + 2 * D_GLA)
D_IN = SPLITS[-1] + GATE_RANK

kernel_name = 'hybrid_conformer_gla_macaron'

def rmsnorm(x, g):
    xf = x.astype(jnp.float32)
    y = xf * lax.rsqrt(jnp.mean(xf * xf, axis=-1, keepdims=True) + EPS)
    return (y * g.astype(jnp.float32)).astype(x.dtype)

def layernorm(x, g, b):
    xf = x.astype(jnp.float32)
    xc = xf - jnp.mean(xf, axis=-1, keepdims=True)
    y = xc * lax.rsqrt(jnp.mean(xc * xc, axis=-1, keepdims=True) + EPS)
    return (y * g.astype(jnp.float32) + b.astype(jnp.float32)).astype(x.dtype)

def modulate(h, shift, scale):
    return h * (1 + scale) + shift

def swiglu(h, w_in, w_out):
    gate, up = jnp.split(h @ w_in, 2, axis=-1)
    return (jax.nn.silu(gate) * up) @ w_out

def conformer_conv(a, b, w_dw, b_dw, g_ln, b_ln):
    u = a * jax.nn.sigmoid(b)
    u = jnp.pad(u, ((0, 0), (CONV_WIDTH - 1, 0), (0, 0)))
    y = lax.conv_general_dilated(u, w_dw.astype(u.dtype)[:, None, :], window_strides=(1,), padding='VALID', dimension_numbers=('NWC', 'WIO', 'NWC'), feature_group_count=D_CONV)
    return jax.nn.silu(layernorm(y + b_dw, g_ln, b_ln))

def gla(q, k, v, r, glr, w_gate_up, b_gate, g_norm):
    bsz, seq, _ = q.shape
    n = seq // CHUNK
    f32 = jnp.float32

    def heads(t, d):
        return t.astype(f32).reshape(bsz, n, CHUNK, GLA_HEADS, d).transpose(0, 3, 1, 2, 4)

    log_a = jax.nn.log_sigmoid((glr @ w_gate_up + b_gate).astype(f32)) / GATE_TAU
    qh = heads(q, GLA_DK) * (GLA_DK ** -0.5)
    kh = heads(k, GLA_DK)
    vh = heads(v, GLA_DV)
    bc = jnp.cumsum(heads(log_a, GLA_DK), axis=3)
    b_end = bc[:, :, :, -1:, :]
    q_fwd = qh * jnp.exp(bc)
    att_fwd = jnp.einsum('bhnik,bhnjk->bhnij', q_fwd, kh * jnp.exp(-bc))
    att_bwd = jnp.einsum('bhnik,bhnjk->bhnij', qh * jnp.exp(-bc), kh * jnp.exp(bc))
    tri = jnp.tril(jnp.ones((CHUNK, CHUNK), dtype=bool))
    o = jnp.einsum('bhnij,bhnjv->bhniv', jnp.where(tri, att_fwd, att_bwd), vh)
    u = jnp.einsum('bhnjk,bhnjv->bhnkv', kh * jnp.exp(b_end - bc), vh)
    g = jnp.exp(b_end[:, :, :, 0, :])

    def step(state, inp):
        g_c, u_c = inp
        return g_c[..., None] * state + u_c, state

    s0 = jnp.zeros((bsz, GLA_HEADS, GLA_DK, GLA_DV), f32)
    _, s_prev = lax.scan(step, s0, (jnp.moveaxis(g, 2, 0), jnp.moveaxis(u, 2, 0)))
    o = o + jnp.einsum('bhnik,nbhkv->bhniv', q_fwd, s_prev)
    o = o * lax.rsqrt(jnp.mean(o * o, axis=-1, keepdims=True) + EPS) * g_norm.astype(f32)[:, None, None, :]
    o = o.transpose(0, 2, 3, 1, 4).reshape(bsz, seq, D_GLA)
    return (o * jax.nn.silu(r.astype(f32))).astype(q.dtype)

def setup_inputs(seed: int = 0) -> dict:
    key = jax.random.key(seed)
    ks = jax.random.split(key, 26)
    L = DEPTH

    def nrm(k, shape, scale):
        return jax.random.normal(k, shape, jnp.float32) * scale

    return {
        'x': nrm(ks[0], (BATCH, SEQ, D_MODEL), 1.0),
        'c': nrm(ks[1], (BATCH, D_MODEL), 1.0),
        'w_ada': nrm(ks[2], (L, D_MODEL, N_MOD * D_MODEL), 0.5 * D_MODEL ** -0.5),
        'b_ada': nrm(ks[3], (L, N_MOD * D_MODEL), 0.02),
        'g_norm_ffn1': 1.0 + nrm(ks[4], (L, D_MODEL), 0.02),
        'w_ffn1_in': nrm(ks[5], (L, D_MODEL, 2 * D_FF), D_MODEL ** -0.5),
        'w_ffn1_out': nrm(ks[6], (L, D_FF, D_MODEL), D_FF ** -0.5),
        'g_norm_mix': 1.0 + nrm(ks[7], (L, D_MODEL), 0.02),
        'w_in': nrm(ks[8], (L, D_MODEL, D_IN), D_MODEL ** -0.5),
        'w_dw': nrm(ks[9], (L, CONV_WIDTH, D_CONV), CONV_WIDTH ** -0.5),
        'b_dw': nrm(ks[10], (L, D_CONV), 0.02),
        'g_conv_ln': 1.0 + nrm(ks[11], (L, D_CONV), 0.02),
        'b_conv_ln': nrm(ks[12], (L, D_CONV), 0.02),
        'w_gate_up': nrm(ks[13], (L, GATE_RANK, GLA_HEADS * GLA_DK), GATE_RANK ** -0.5),
        'b_gate': nrm(ks[14], (L, GLA_HEADS * GLA_DK), 0.02),
        'g_gla_norm': 1.0 + nrm(ks[15], (L, GLA_HEADS, GLA_DV), 0.02),
        'w_out': nrm(ks[16], (L, D_MIX, D_MODEL), D_MIX ** -0.5),
        'g_norm_ffn2': 1.0 + nrm(ks[17], (L, D_MODEL), 0.02),
        'w_ffn2_in': nrm(ks[18], (L, D_MODEL, 2 * D_FF), D_MODEL ** -0.5),
        'w_ffn2_out': nrm(ks[19], (L, D_FF, D_MODEL), D_FF ** -0.5),
        'g_norm_final': 1.0 + nrm(ks[20], (D_MODEL,), 0.02),
        'w_ada_final': nrm(ks[21], (D_MODEL, 2 * D_MODEL), 0.5 * D_MODEL ** -0.5),
        'b_ada_final': nrm(ks[22], (2 * D_MODEL,), 0.02),
    }

def reference(x, c, w_ada, b_ada, g_norm_ffn1, w_ffn1_in, w_ffn1_out, g_norm_mix, w_in, w_dw, b_dw, g_conv_ln, b_conv_ln, w_gate_up, b_gate, g_gla_norm, w_out, g_norm_ffn2, w_ffn2_in, w_ffn2_out, g_norm_final, w_ada_final, b_ada_final):
    bsz = x.shape[0]
    c_act = jax.nn.silu(c)
    for l in range(DEPTH):
        mod = (c_act @ w_ada[l] + b_ada[l]).reshape(bsz, N_MOD, 1, D_MODEL)
        h = modulate(rmsnorm(x, g_norm_ffn1[l]), mod[:, 0], mod[:, 1])
        x = x + 0.5 * mod[:, 2] * swiglu(h, w_ffn1_in[l], w_ffn1_out[l])
        h = modulate(rmsnorm(x, g_norm_mix[l]), mod[:, 3], mod[:, 4])
        a, b, q, k, v, r, glr = jnp.split(h @ w_in[l], SPLITS, axis=-1)
        y_conv = conformer_conv(a, b, w_dw[l], b_dw[l], g_conv_ln[l], b_conv_ln[l])
        y_gla = gla(q, k, v, r, glr, w_gate_up[l], b_gate[l], g_gla_norm[l])
        x = x + mod[:, 5] * (jnp.concatenate([y_conv, y_gla], axis=-1) @ w_out[l])
        h = modulate(rmsnorm(x, g_norm_ffn2[l]), mod[:, 6], mod[:, 7])
        x = x + 0.5 * mod[:, 8] * swiglu(h, w_ffn2_in[l], w_ffn2_out[l])
    fmod = (c_act @ w_ada_final + b_ada_final).reshape(bsz, 2, 1, D_MODEL)
    return modulate(rmsnorm(x, g_norm_final), fmod[:, 0], fmod[:, 1])


_drawn_inputs = setup_inputs


def setup_inputs(seed=0):
    import zlib

    import numpy as np

    out = dict(_drawn_inputs(seed))
    spreads = {}
    factors = {'g_norm_ffn1': 8.0,
     'g_norm_mix': 6.582,
     'b_dw': 53.677,
     'g_conv_ln': 64.0,
     'b_conv_ln': 64.0,
     'b_gate': 8.0,
     'g_gla_norm': 8.0,
     'g_norm_ffn2': 8.0,
     'g_norm_final': 9.134,
     'b_ada_final': 2.767}
    for name, (base, spread) in spreads.items():
        noise = np.random.default_rng([zlib.crc32(name.encode()), seed]).standard_normal(out[name].shape)
        drawn = base * np.exp(spread * noise) if base else spread * noise
        out[name] = jnp.asarray(drawn.astype(out[name].dtype))
    for name, factor in factors.items():
        out[name] = (out[name] * factor).astype(out[name].dtype)
    return out
```

```python
from contextlib import ExitStack

import concourse.bass as bass
from concourse import mybir

F32 = mybir.dt.float32
F32R = mybir.dt.float32r
U32 = mybir.dt.uint32
ALU = mybir.AluOpType
ACT = mybir.ActivationFunctionType

P = 128
LAYERS = 2
D = 1024
T = 512
DK = D // P
D_FF = 2816
FK = D_FF // P
N_MOD = 9
EPS = 1e-6
HEADS = 4
CHUNK = 64
NCHUNK = T // CHUNK
TB = T // P
TAPS = 31
CK = 4
RANK = 16
TAU = 16.0
D_IN = 2576

KU, CU = 4, 256
AHEAD = 4
BLOCKS = D_FF // CU
PAIRS = D // CU
OUT_UNITS = -(-FK // KU)
IN_UNITS = 4 * BLOCKS
FFN_UNITS = IN_UNITS + PAIRS * OUT_UNITS
ZIN_UNITS = 20
MIX_UNITS = ZIN_UNITS + 2 * PAIRS
LAYER_UNITS = 2 * FFN_UNITS + MIX_UNITS
FFN_BASE = (0, FFN_UNITS + MIX_UNITS)
MIX_BASE = FFN_UNITS
ZIN_COLS = (0, 512, 256, 768, 1024, 1280, 1536, 1792, 2048, 2304)
GLR_COL = 2560
assert IN_UNITS % AHEAD == 0 and (PAIRS * OUT_UNITS) % AHEAD == 0 and MIX_UNITS % AHEAD == 0
assert BLOCKS % 2 == 1 and OUT_UNITS * 2 % AHEAD == 0

ADA_PRE = 2
ADA_SLOTS = 2
ADA_IN = (BLOCKS - 1) // 2
ADA_OUT = PAIRS // 2
assert ADA_IN + 2 * ADA_OUT == N_MOD


def trunk(nc, xT, cT, w_ada, b_adaT, g_normT, w_ffn1_in, w_ffn1_out, w_in, w_glr, w_ffn2_in, w_ffn2_out, w_out,
          w_dwT, mix_colsT, w_gate_up, outT):
    ffn_in = [w.rearrange("l (c k p) n -> p (l c) k n", p=P, k=KU) for w in (w_ffn1_in, w_ffn2_in)]
    ffn_out = [w.rearrange("l (k p) n -> p (l k) n", p=P) for w in (w_ffn1_out, w_ffn2_out)]
    z_in = w_in.rearrange("l (c k p) n -> p (l c) k n", p=P, k=KU)
    y_out = w_out.rearrange("l (c k p) n -> p (l c) k n", p=P, k=KU)
    ada = w_ada.rearrange("(k p) n -> p k n", p=P)

    with ExitStack() as ctx:
        def sem(name):
            return ctx.enter_context(nc.semaphore(name))

        top = [-(-nc.sbuf_base // 64) * 64]

        def place(name, shape, dt=F32, at=None):
            size = 1
            for n in shape[1:]:
                size *= n
            size *= 4
            off = top[0] if at is None else at[0]
            (top if at is None else at)[0] = off + -(-size // 32) * 32
            return nc.alloc_sbuf_tensor_at(name, shape, dt, offset=off)

        x = place("x", [P, DK, T])
        h_hi = place("h_hi", [P, DK, T], F32R)
        h_lo = place("h_lo", [P, DK, T], F32R)
        raw = place("raw", [P, AHEAD, KU, CU])
        w_hi = place("w_hi", [P, AHEAD, KU, CU], F32R)
        w_lo = place("w_lo", [P, AHEAD, KU, CU], F32R)
        ada_raw = place("ada_raw", [P, ADA_SLOTS, D])
        ada_acc = place("ada_acc", [P, D])
        tmp = place("tmp", [P, 3, T])
        ssq = place("ssq", [P, T])
        ones = place("ones", [P, P])
        eps = place("eps", [P, 1])
        ident = place("ident", [P, P])
        mask_f = place("mask_f", [P, P])
        mask_b = place("mask_b", [P, P])
        mod = place("mod", [P, N_MOD, DK])
        b_ada = place("b_ada", [P, LAYERS * N_MOD + 2, DK])
        g_norm = place("g_norm", [P, 3 * LAYERS + 1, DK])
        gain = place("gain", [P, DK])
        gate = place("gate", [P, DK])
        c_act = place("c_act", [P, DK])
        shared = top[0]
        ffn_map = [shared]
        g_hi = place("g_hi", [P, FK, T], F32R, ffn_map)
        g_lo = place("g_lo", [P, FK, T], F32R, ffn_map)
        pre_map = [shared]
        pre = place("pre", [P, ADA_PRE, DK, D], F32, pre_map)
        mix_map = [shared]
        PAD = TAPS - 1
        glu = place("glu", [P, CK, PAD + T], F32, mix_map)
        conv = place("conv", [P, CK, T], F32, mix_map)
        bc = place("bc", [P, 2, T], F32, mix_map)
        k_bwd = place("k_bwd", [P, 2, T], F32, mix_map)
        k_fwd = place("k_fwd", [P, 2, T], F32, mix_map)
        k_end = place("k_end", [P, 2, T], F32, mix_map)
        q_fwd = place("q_fwd", [P, 2, T], F32, mix_map)
        q_bwd = place("q_bwd", [P, 2, T], F32, mix_map)
        v = place("v", [P, TB, HEADS * P], F32, mix_map)
        att = place("att", [P, HEADS, T], F32, mix_map)
        k_endT = place("k_endT", [P, 2, T], F32, mix_map)
        h_full = place("h_full", [P, 3, T], F32, [mix_map[0]])
        state = place("state", [P, 2, NCHUNK - 1, P], F32, mix_map)
        r_act = place("r_act", [P, HEADS, T], F32, mix_map)
        end_exp = place("end_exp", [P, 2, NCHUNK], F32, mix_map)
        w_dw = place("w_dw", [P, CK, TAPS], F32, mix_map)
        cols = place("cols", [P, 18], F32, mix_map)
        glr_raw = place("glr_raw", [P, DK, RANK], F32, mix_map)
        glr_hi = place("glr_hi", [P, DK, RANK], F32R, mix_map)
        glr_lo = place("glr_lo", [P, DK, RANK], F32R, mix_map)
        glr = place("glr", [RANK, T], F32, mix_map)
        up_w = place("up_w", [RANK, 2 * P], F32, mix_map)
        restart = place("restart", [P, T], F32, mix_map)
        assert max(ffn_map[0], pre_map[0], mix_map[0]) <= nc.sbuf_usable_end, (ffn_map, pre_map, mix_map)
        b_dw, g_ln, b_ln, b_gate, g_gla = (cols[:, a:b] for a, b in ((0, 4), (4, 8), (8, 12), (12, 14), (14, 18)))

        bank = [ctx.enter_context(nc.psum_tensor(f"bank{i}", [P, T], F32)) for i in range(8)]
        IN_GATE, IN_UP, OUT_A, OUT_B = (0, 1), (2, 3), (4, 5), (6, 7)
        ADA_BANK_IN, ADA_BANK_OUT, STAT = 7, 0, 1

        w_loaded = [sem(f"w_loaded{s}") for s in range(AHEAD)]
        w_round = sem("w_round")
        w_split = sem("w_split")
        w_used = sem("w_used")
        par_loaded = sem("par_loaded")
        pre_loaded = [sem(f"pre_loaded{b}") for b in range(ADA_PRE * DK)]
        x_loaded = sem("x_loaded")
        mixp_loaded = sem("mixp_loaded")
        ada_loaded = [sem(f"ada_loaded{s}") for s in range(ADA_SLOTS)]
        ada_mac = sem("ada_mac")
        ada_sum = sem("ada_sum")
        mod_ready = sem("mod_ready")
        pre_mac = sem("pre_mac")
        c_ready = sem("c_ready")
        const_ready = sem("const_ready")
        x_ready = sem("x_ready")
        sq_ready = sem("sq_ready")
        ssq_ready = sem("ssq_ready")
        stat_ready = sem("stat_ready")
        rms_root = sem("rms_root")
        rms_step = sem("rms_step")
        gain_ready = sem("gain_ready")
        xn_ready = sem("xn_ready")
        h_round = sem("h_round")
        h_ready = sem("h_ready")
        silu_done = sem("silu_done")
        g_ready = sem("g_ready")
        g_round = sem("g_round")
        g_split = sem("g_split")
        gate_ready = sem("gate_ready")
        final_ready = sem("final_ready")
        stored = sem("stored")
        built = sem("built")
        sig_done = sem("sig_done")
        glu_done = sem("glu_done")
        tap_done = sem("tap_done")
        glrw_round = sem("glrw_round")
        glrw_split = sem("glrw_split")
        glr_done = sem("glr_done")
        glr_out = sem("glr_out")
        z_done = sem("z_done")
        soft = sem("soft")
        logsig = sem("logsig")
        scanned = sem("scanned")
        diff = sem("diff")
        exps = sem("exps")
        qk_done = sem("qk_done")
        v_out = sem("v_out")
        r_out = sem("r_out")
        att_mm = sem("att_mm")
        att_sel = sem("att_sel")
        kT_mm = sem("kT_mm")
        kT_out = sem("kT_out")
        u_mm = sem("u_mm")
        st = sem("st")
        o_mm = sem("o_mm")
        o_sq = sem("o_sq")
        oss_mm = sem("oss_mm")
        o_root = sem("o_root")
        o_norm = sem("o_norm")
        y_round = sem("y_round")
        y_ready = sem("y_ready")
        mean_mm = sem("mean_mm")
        centred = sem("centred")
        c_sq = sem("c_sq")
        var_mm = sem("var_mm")
        ln_root = sem("ln_root")
        ln_step = sem("ln_step")
        c_act_done = sem("c_act_done")

        BUILDS = 4
        CONSTS = 11

        def o_square(h):
            return (q_bwd if h < 2 else k_fwd)[:, h % 2, :]

        block = ctx.enter_context(nc.Block())

        @block.sync
        def _(sp):
            sp.dma_start(c_act[:], cT).then_inc(par_loaded, 16)
            sp.dma_start(b_ada[:], b_adaT).then_inc(par_loaded, 16)
            sp.dma_start(g_norm[:], g_normT).then_inc(par_loaded, 16)
            sp.dma_start(x[:], xT.rearrange("(k p) t -> p k t", p=P)).then_inc(x_loaded, 16)
            for b in range(ADA_PRE):
                for k in range(DK):
                    sp.dma_start(pre[:, b, k, :], ada[:, k, b * D:(b + 1) * D]).then_inc(pre_loaded[b * DK + k], 16)

            def load(unit, slot, src, tiles=KU):
                sp.wait_ge(w_split, unit + 1)
                sp.dma_start(raw[:, slot, 0:tiles, :], src).then_inc(w_loaded[slot], 16)

            def load_block(l, f, base, b, s):
                for half in range(2):
                    for c in range(2):
                        load(base + 4 * b + 2 * half + c, (s + 2 * half + c) % AHEAD,
                             ffn_in[f][:, 2 * l + c, :, bass.ds(b * CU + half * D_FF, CU)])

            def load_ffn(l, f):
                base = l * LAYER_UNITS + FFN_BASE[f]
                load_block(l, f, base, 0, 0)
                with sp.Fori(0, (BLOCKS - 1) // 2) as j:
                    for i in range(2):
                        load_block(l, f, base, 2 * j + 1 + i, 0)
                with sp.Fori(0, PAIRS // 2) as j:
                    for i in range(2):
                        for n in range(OUT_UNITS):
                            tiles = min(KU, FK - n * KU)
                            q = i * OUT_UNITS + n
                            load(base + IN_UNITS + j * 2 * OUT_UNITS + q, q % AHEAD,
                                 ffn_out[f][:, bass.ds(l * FK + n * KU, tiles), bass.ds((2 * j + i) * CU, CU)], tiles)

            with sp.Fori(0, LAYERS) as l:
                load_ffn(l, 0)
                base = l * LAYER_UNITS + MIX_BASE
                for n, col in enumerate(ZIN_COLS):
                    for c in range(2):
                        load(base + 2 * n + c, (2 * n + c) % AHEAD, z_in[:, 2 * l + c, :, col:col + CU])
                for n in range(PAIRS):
                    for i, c in enumerate((1, 0)):
                        load(base + ZIN_UNITS + 2 * n + i, (2 * n + i) % AHEAD,
                             y_out[:, 2 * l + c, :, n * CU:(n + 1) * CU])
                load_ffn(l, 1)
            load_block(0, 0, LAYERS * LAYER_UNITS, 0, 0)
            for k in range(DK):
                sp.wait_ge(final_ready, k + 1)
                sp.dma_start(outT[k * P:(k + 1) * P, :], x[:, k, :]).then_inc(stored, 16)
            sp.wait_ge(stored, 16 * DK)

        @block.gpsimd
        def _(pool):
            def load_ada(blk):
                for k in range(DK):
                    pool.wait_ge(ada_mac, (blk - ADA_PRE) * DK + k + 1)
                    pool.dma_start(ada_raw[:, k % ADA_SLOTS, :],
                                   ada[:, k, bass.ds(blk * D, D)]).then_inc(ada_loaded[k % ADA_SLOTS], 16)

            pool.memset(eps[:], EPS).then_inc(const_ready, 1)
            pool.memset(ones[:], 1.0).then_inc(const_ready, 1)
            pool.memset(mask_f[:], 1.0).then_inc(const_ready, 1)
            pool.memset(mask_b[:], 1.0).then_inc(const_ready, 1)
            pool.memset(ident[:], 0.0).then_inc(const_ready, 1)
            pool.wait_ge(const_ready, 5)
            pool.affine_select(out=ident[:], in_=ident[:], compare_op=ALU.not_equal, fill=1.0, base=0,
                               pattern=[[-1, P]], channel_multiplier=1).then_inc(const_ready, 1)
            pool.affine_select(out=mask_f[:], in_=mask_f[:], compare_op=ALU.is_ge, fill=0.0, base=0,
                               pattern=[[1, P]], channel_multiplier=-1).then_inc(const_ready, 1)
            pool.affine_select(out=mask_b[:], in_=mask_b[:], compare_op=ALU.is_ge, fill=0.0, base=-1,
                               pattern=[[-1, P]], channel_multiplier=1).then_inc(const_ready, 1)
            pool.wait_ge(const_ready, 8)
            pool.memset(mask_f[0:CHUNK, CHUNK:P], 0.0).then_inc(const_ready, 1)
            pool.memset(mask_b[CHUNK:P, 0:CHUNK], 0.0).then_inc(const_ready, 1)
            pool.memset(mask_b[0:CHUNK, CHUNK:P], 0.0).then_inc(const_ready, 1)
            with pool.Fori(0, LAYERS) as l:
                with pool.Fori(0, ADA_IN) as j:
                    load_ada(l * N_MOD + j + ADA_PRE)
                with pool.Fori(0, ADA_OUT) as j:
                    load_ada(l * N_MOD + j + (ADA_PRE + ADA_IN))
                pool.wait_ge(w_used, l * LAYER_UNITS + MIX_BASE)
                pool.dma_start(w_dw[:], w_dwT[:, bass.ds(l, 1), :, :].rearrange("p l c t -> p (l c) t")).then_inc(mixp_loaded, 16)
                pool.dma_start(cols[:], mix_colsT[:, bass.ds(l, 1), :].rearrange("p l c -> p (l c)")).then_inc(mixp_loaded, 16)
                pool.dma_start(glr_raw[:], w_glr[:, bass.ds(l * DK, DK), :]).then_inc(mixp_loaded, 16)
                pool.dma_start(up_w[:], w_gate_up[:, bass.ds(l, 1), :].rearrange("r l c -> r (l c)")).then_inc(mixp_loaded, 16)
                pool.memset(glu[:, :, 0:PAD], 0.0).then_inc(built, 1)
                pool.memset(att[:], 0.0).then_inc(built, 1)
                by_chunk = restart[:].rearrange("p (c j) -> p c j", j=CHUNK)
                pool.memset(by_chunk[:, :, 0:1], 0.0).then_inc(built, 1)
                pool.memset(by_chunk[:, :, 1:CHUNK], 1.0).then_inc(built, 1)
                with pool.Fori(0, ADA_OUT) as j:
                    load_ada(l * N_MOD + j + (ADA_PRE + ADA_IN + ADA_OUT))

        @block.tensor
        def _(pe):
            def three(out, a_hi, a_lo, b_hi, b_lo, first, last):
                nc.tensor.matmul(out, a_hi, b_hi, start=first, stop=False)
                nc.tensor.matmul(out, a_hi, b_lo, start=False, stop=False)
                return nc.tensor.matmul(out, a_lo, b_hi, start=False, stop=last)

            def unit(u, slot, banks, rhs_hi, rhs_lo, k0, total, tiles=KU, k_wait=None):
                pe.wait_ge(w_split, u + 1 + AHEAD)
                for k in range(tiles):
                    if k_wait is not None:
                        pe.wait_ge(k_wait[0], k_wait[1] + k + 1)
                    for m in range(2):
                        mm = three(bank[banks[m]][:], w_hi[:, slot, k, m * P:(m + 1) * P], w_lo[:, slot, k, m * P:(m + 1) * P],
                                   rhs_hi[:, k0 + k, :], rhs_lo[:, k0 + k, :], k0 + k == 0, k0 + k == total - 1)
                mm.then_inc(w_used, 1)

            def ada_flush(blk, into):
                pe.wait_ge(ada_mac, (blk - ADA_PRE + 1) * DK + ADA_SLOTS)
                pe.wait_ge(mod_ready, blk)
                for n in range(DK):
                    mm = nc.tensor.matmul(bank[into][:, n:n + 1], ada_acc[:, n * P:(n + 1) * P], ones[:, 0:1],
                                          start=True, stop=True)
                mm.then_inc(ada_sum, 1)

            def stat(n):
                pe.wait_ge(ssq_ready, (n + 1) * DK)
                nc.tensor.matmul(bank[STAT][:], ones[:], ssq[:], start=True, stop=True).then_inc(stat_ready, 1)

            def ffn(l, f):
                n = l * 3 + 2 * f
                base = l * LAYER_UNITS + FFN_BASE[f]
                done = (l * 2 + f) * FK
                stat(n)

                def in_block(b, first):
                    if not first:
                        pe.wait_ge(silu_done, done + 2 * b)
                    for c in range(2):
                        unit(base + 4 * b + c, c, IN_GATE, h_hi, h_lo, c * KU, DK,
                             k_wait=(h_ready, n * DK + c * KU) if first else None)
                    if not first:
                        pe.wait_ge(g_ready, done + 2 * b)
                    for c in range(2):
                        unit(base + 4 * b + 2 + c, 2 + c, IN_UP, h_hi, h_lo, c * KU, DK)

                in_block(0, True)
                with pe.Fori(0, (BLOCKS - 1) // 2) as j:
                    for i in range(2):
                        in_block(2 * j + 1 + i, False)
                    if f == 0:
                        ada_flush(l * N_MOD + j + ADA_PRE, ADA_BANK_IN)
                with pe.Fori(0, PAIRS // 2) as j:
                    for i in range(2):
                        banks = (OUT_A, OUT_B)[i]
                        pe.wait_ge(x_ready, l * 3 * DK + 2 * f * DK + 4 * j + 2 * i + DK - 2)
                        if i == 1:
                            pe.wait_ge(mod_ready, l * N_MOD + ADA_PRE + ADA_IN + f * ADA_OUT)
                        for m in range(OUT_UNITS):
                            tiles = min(KU, FK - m * KU)
                            q = i * OUT_UNITS + m
                            unit(base + IN_UNITS + j * 2 * OUT_UNITS + q, q % AHEAD, banks, g_hi, g_lo, m * KU, FK,
                                 tiles, k_wait=(g_split, done + m * KU) if i == 0 else None)
                    ada_flush(l * N_MOD + j + ADA_PRE + ADA_IN + f * ADA_OUT, ADA_BANK_OUT)

            def mixer(l):
                n = l * 3 + 1
                base = l * LAYER_UNITS + MIX_BASE
                stat(n)
                for i in range(4):
                    for c in range(2):
                        unit(base + 2 * i + c, (2 * i + c) % AHEAD, (2 * i, 2 * i + 1), h_hi, h_lo, c * KU, DK,
                             k_wait=(h_ready, n * DK + c * KU) if i == 0 else None)
                pe.wait_ge(glrw_split, l + 1)
                pe.wait_ge(glu_done, l * CK + 2)
                for k in range(DK):
                    mm = three(bank[0][0:RANK, :], glr_hi[:, k, :], glr_lo[:, k, :], h_hi[:, k, :], h_lo[:, k, :],
                               k == 0, k == DK - 1)
                mm.then_inc(glr_done, 1)
                for c in range(2):
                    unit(base + 8 + c, c, (2, 3), h_hi, h_lo, c * KU, DK)
                pe.wait_ge(glr_out, l + 1)
                for t in range(2):
                    mm = nc.tensor.matmul(bank[t][:], up_w[:, t * P:(t + 1) * P], glr[:], start=True, stop=True)
                    mm.then_inc(z_done, 1)
                pe.wait_ge(glu_done, l * CK + CK)
                for c in range(2):
                    unit(base + 10 + c, 2 + c, (4, 5), h_hi, h_lo, c * KU, DK)
                pe.wait_ge(soft, l * 8 + 2)
                vbank = (6, 7, 0, 1)
                for half in range(2):
                    for c in range(2):
                        pe.wait_ge(w_split, base + 12 + 2 * half + c + 1 + AHEAD)
                        slot = 2 * half + c
                        for tb in range(TB):
                            for k in range(KU):
                                kk = c * KU + k
                                mm = three(bank[vbank[tb]][:, half * CU:(half + 1) * CU],
                                           h_hi[:, kk, tb * P:(tb + 1) * P], h_lo[:, kk, tb * P:(tb + 1) * P],
                                           w_hi[:, slot, k, :], w_lo[:, slot, k, :], kk == 0, kk == DK - 1)
                        mm.then_inc(w_used, 1)
                pe.wait_ge(qk_done, l * 10 + 4)
                for c in range(2):
                    unit(base + 16 + c, c, (2, 3), h_hi, h_lo, c * KU, DK)
                pe.wait_ge(qk_done, l * 10 + 10)
                pe.wait_ge(v_out, l * TB + TB)

                def scores(h):
                    t, s = h // 2, h % 2
                    rows = slice(CHUNK * s, CHUNK * s + CHUNK)
                    fwd, bwd = (6, 7) if s == 0 else (0, 1)
                    if h >= 2:
                        pe.wait_ge(att_sel, l * 8 + 4)
                    for kk, qq, into in ((k_fwd, q_fwd, fwd), (k_bwd, q_bwd, bwd)):
                        for b in range(TB):
                            mm = nc.tensor.matmul(bank[into][:, b * P:(b + 1) * P], kk[rows, t, b * P:(b + 1) * P],
                                                  qq[rows, t, b * P:(b + 1) * P], start=True, stop=True)
                    mm.then_inc(att_mm, 1)

                scores(0)
                scores(1)
                for c in range(2):
                    unit(base + 18 + c, 2 + c, (4, 5), h_hi, h_lo, c * KU, DK)
                scores(2)
                scores(3)
                pe.wait_ge(r_out, l * HEADS + HEADS)
                for t in range(2):
                    for b in range(TB):
                        mm = nc.tensor.transpose(bank[2 + t][:, b * P:(b + 1) * P], k_end[:, t, b * P:(b + 1) * P], ident[:])
                    mm.then_inc(kT_mm, 1)
                pe.wait_ge(att_sel, l * 8 + 8)
                pe.wait_ge(kT_out, l * 2 + 2)
                for h in range(HEADS):
                    for b in range(TB):
                        nc.tensor.matmul(bank[h][:, b * P:(b + 1) * P], v[:, b, h * P:(h + 1) * P],
                                         att[:, h, b * P:(b + 1) * P], start=b == 0, stop=False, skip_group_check=True)
                for t in range(2):
                    for odd in range(2):
                        for s in range(2):
                            for b in range(TB - odd):
                                rows = slice(CHUNK * odd, CHUNK * odd + CHUNK)
                                mm = nc.tensor.matmul(
                                    bank[4 + 2 * t + odd][CHUNK * s:CHUNK * s + CHUNK, b * P:(b + 1) * P],
                                    k_endT[rows, t, b * P + CHUNK * s:b * P + CHUNK * s + CHUNK],
                                    v[rows, b, (2 * t + s) * P:(2 * t + s + 1) * P], start=True, stop=True)
                    mm.then_inc(u_mm, 1)
                for h in range(HEADS):
                    t, s = h // 2, h % 2
                    rows = slice(CHUNK * s, CHUNK * s + CHUNK)
                    pe.wait_ge(st, (l * 2 + t + 1) * (NCHUNK - 1))
                    for c in range(1, NCHUNK):
                        mm = nc.tensor.matmul(bank[h][:, c * CHUNK:(c + 1) * CHUNK], state[rows, t, c - 1, :],
                                              q_fwd[rows, t, c * CHUNK:(c + 1) * CHUNK], start=False, stop=c == NCHUNK - 1,
                                              skip_group_check=True)
                    mm.then_inc(o_mm, 1)
                for h in range(HEADS):
                    pe.wait_ge(o_sq, l * HEADS + h + 1)
                    nc.tensor.matmul(bank[4 + h][:], ones[:], o_square(h), start=True, stop=True).then_inc(oss_mm, 1)
                pe.wait_ge(tap_done, (l + 1) * TAPS * CK)
                pe.wait_ge(o_root, l * HEADS + 2)
                for i in range(CK):
                    mm = nc.tensor.matmul(bank[4][:], ones[:], conv[:, i, :], start=i == 0, stop=i == CK - 1)
                mm.then_inc(mean_mm, 1)
                for i in range(CK):
                    pe.wait_ge(c_sq, l * CK + i + 1)
                    mm = nc.tensor.matmul(bank[5][:], ones[:], glu[:, i, PAD:PAD + T], start=i == 0, stop=i == CK - 1)
                mm.then_inc(var_mm, 1)
                pe.wait_ge(y_ready, l * DK + HEADS)
                for p_ in range(PAIRS):
                    if p_ == 2:
                        pe.wait_ge(ln_root, l + 1)
                    for i, c in enumerate((1, 0)):
                        u = base + ZIN_UNITS + 2 * p_ + i
                        if i == 1 and p_ == 0:
                            pe.wait_ge(y_ready, l * DK + DK)
                        slot = (2 * p_ + i) % AHEAD
                        pe.wait_ge(w_split, u + 1 + AHEAD)
                        for k in range(KU):
                            for m in range(2):
                                mm = three(bank[2 * p_ + m][:], w_hi[:, slot, k, m * P:(m + 1) * P],
                                           w_lo[:, slot, k, m * P:(m + 1) * P], h_hi[:, c * KU + k, :], h_lo[:, c * KU + k, :],
                                           i == 0 and k == 0, i == 1 and k == KU - 1)
                        mm.then_inc(w_used, 1)

            pe.wait_ge(const_ready, CONSTS)
            for b in range(ADA_PRE):
                if b:
                    pe.wait_ge(mod_ready, b)
                pe.wait_ge(pre_mac, (b + 1) * DK)
                for n in range(DK):
                    mm = nc.tensor.matmul(bank[ADA_BANK_IN][:, n:n + 1], ada_acc[:, n * P:(n + 1) * P], ones[:, 0:1],
                                          start=True, stop=True)
                mm.then_inc(ada_sum, 1)
            with pe.Fori(0, LAYERS) as l:
                ffn(l, 0)
                mixer(l)
                ffn(l, 1)
            stat(3 * LAYERS)

        @block.scalar
        def _(act):
            def split(grp, q, tiles=KU, used=True):
                grp, slot = grp + q // AHEAD, q % AHEAD
                act.wait_ge(w_loaded[slot], grp * 16 + 16)
                if used:
                    act.wait_ge(w_used, grp * AHEAD + slot - AHEAD + 1)
                nc.scalar.activation(w_hi[:, slot, 0:tiles, :], raw[:, slot, 0:tiles, :], ACT.Copy).then_inc(w_round, 1)

            def root(n):
                act.wait_ge(stat_ready, n + 1)
                nc.scalar.activation(ssq[:], bank[STAT][:], ACT.Sqrt, bias=eps[:, 0:1], scale=1.0 / D).then_inc(rms_root, 1)

            def norm(n, shift):
                root(n)
                act.wait_ge(gain_ready, n + 1)
                for k in range(DK):
                    act.wait_ge(xn_ready, n * DK + k + 1)
                    t = tmp[:, k % 3, :]
                    nc.scalar.activation(h_hi[:, k, :], t, ACT.Identity, bias=mod[:, shift, k:k + 1], scale=gain[:, k:k + 1])
                    if k >= 3:
                        act.wait_ge(h_ready, n * DK + k - 2)
                    nc.scalar.activation(h_full[:, k % 3, :], t, ACT.Identity, bias=mod[:, shift, k:k + 1],
                                         scale=gain[:, k:k + 1]).then_inc(h_round, 1)

            def square(m, slot, x_at, ssq_at):
                act.wait_ge(x_ready, x_at)
                if ssq_at is not None:
                    act.wait_ge(ssq_ready, ssq_at)
                nc.scalar.activation(tmp[:, slot, :], x[:, bass.ds(m, 1), :].rearrange("p k t -> p (k t)"),
                                     ACT.Square).then_inc(sq_ready, 1)

            def ffn(l, f):
                n = l * 3 + 2 * f
                grp = l * (LAYER_UNITS // AHEAD) + FFN_BASE[f] // AHEAD
                done = (l * 2 + f) * FK
                norm(n, 6 * f)

                def in_block(b, first):
                    split(grp + b, AHEAD)
                    split(grp + b, AHEAD + 1)
                    if first:
                        act.wait_ge(h_ready, n * DK + DK)
                    else:
                        act.wait_ge(g_split, done + 2 * b)
                    for i in range(2):
                        nc.scalar.activation(tmp[:, i, :], bank[IN_GATE[i]][:], ACT.Silu).then_inc(silu_done, 1)
                    split(grp + b, AHEAD + 2)
                    split(grp + b, AHEAD + 3)
                    for i in range(2):
                        act.wait_ge(g_ready, done + 2 * b + i + 1)
                        nc.scalar.activation(g_hi[:, bass.ds(2 * b + i, 1), :].rearrange("p k t -> p (k t)"), tmp[:, i, :],
                                             ACT.Copy).then_inc(g_round, 1)

                in_block(0, True)
                with act.Fori(0, (BLOCKS - 1) // 2) as j:
                    for i in range(2):
                        in_block(2 * j + 1 + i, False)
                act.wait_ge(g_split, done + FK)
                with act.Fori(0, PAIRS // 2) as j:
                    for i in range(2):
                        for m in range(OUT_UNITS):
                            q = i * OUT_UNITS + m + AHEAD
                            tiles = FK % KU if q % OUT_UNITS == OUT_UNITS - 1 else KU
                            split(grp + BLOCKS + j * (2 * OUT_UNITS // AHEAD), q, tiles)
                        for t in range(2):
                            m = 4 * j + 2 * i + t
                            square(m, t, DK + l * 3 * DK + 2 * f * DK + m + 1, (n + 1) * DK + m - 1)

            def mixer(l):
                n = l * 3 + 1
                grp = l * (LAYER_UNITS // AHEAD) + MIX_BASE // AHEAD

                def step(u):
                    split(grp, u + AHEAD)

                def round_head(h):
                    act.wait_ge(o_norm, l * 12 + 3 * h + 3)
                    nc.scalar.activation(h_hi[:, CK + h, :], v[:, h, :], ACT.Copy).then_inc(y_round, 1)

                norm(n, 3)
                step(0)
                step(1)
                act.wait_ge(mixp_loaded, l * 64 + 64)
                nc.scalar.activation(glr_hi[:], glr_raw[:], ACT.Copy).then_inc(glrw_round, 1)
                step(2)
                step(3)
                act.wait_ge(h_ready, n * DK + DK)
                for i in range(2):
                    nc.scalar.activation(tmp[:, i, :], bank[2 + i][:], ACT.Sigmoid).then_inc(sig_done, 1)
                for u in range(4, 8):
                    step(u)
                act.wait_ge(glu_done, l * CK + 2)
                for i in range(2):
                    nc.scalar.activation(tmp[:, i, :], bank[6 + i][:], ACT.Sigmoid).then_inc(sig_done, 1)
                act.wait_ge(glr_done, l + 1)
                nc.scalar.activation(glr[:], bank[0][0:RANK, :], ACT.Copy).then_inc(glr_out, 1)
                step(8)
                step(9)
                act.wait_ge(z_done, l * 2 + 2)
                for t in range(2):
                    nc.scalar.activation(k_fwd[:, t, :], bank[t][:], ACT.Identity, bias=b_gate[:, t:t + 1]).then_inc(soft, 1)
                for t in range(2):
                    act.wait_ge(soft, l * 8 + 1 + t)
                    nc.scalar.activation(k_bwd[:, t, :], k_fwd[:, t, :], ACT.Abs).then_inc(soft, 1)
                for t in range(2):
                    act.wait_ge(soft, l * 8 + 3 + t)
                    nc.scalar.activation(k_bwd[:, t, :], k_bwd[:, t, :], ACT.Exp, scale=-1.0).then_inc(soft, 1)
                for t in range(2):
                    act.wait_ge(soft, l * 8 + 5 + t)
                    nc.scalar.activation(k_bwd[:, t, :], k_bwd[:, t, :], ACT.Ln, bias=1.0).then_inc(soft, 1)
                step(10)
                for t in range(2):
                    act.wait_ge(diff, l * 2 + t + 1)
                    ends = bc[:, t, :].rearrange("p (c j) -> p c j", j=CHUNK)[:, :, CHUNK - 1:CHUNK]
                    nc.scalar.activation(k_bwd[:, t, :], bc[:, t, :], ACT.Exp, scale=1.0 / TAU).then_inc(exps, 1)
                    nc.scalar.activation(k_fwd[:, t, :], bc[:, t, :], ACT.Exp, scale=-1.0 / TAU).then_inc(exps, 1)
                    nc.scalar.activation(k_end[:, t, :], k_end[:, t, :], ACT.Exp, scale=1.0 / TAU).then_inc(exps, 1)
                    nc.scalar.activation(end_exp[:, t, :], ends, ACT.Exp, scale=1.0 / TAU).then_inc(exps, 1)
                for u in range(11, 16):
                    step(u)
                for tb, b in enumerate((6, 7, 0, 1)):
                    nc.scalar.activation(v[:, tb, :], bank[b][:], ACT.Copy).then_inc(v_out, 1)
                for p_ in range(2):
                    step(16 + 2 * p_)
                    step(17 + 2 * p_)
                    for i in range(2):
                        nc.scalar.activation(r_act[:, 2 * p_ + i, :], bank[2 + 2 * p_ + i][:], ACT.Silu).then_inc(r_out, 1)
                for t in range(2):
                    act.wait_ge(kT_mm, l * 2 + t + 1)
                    nc.scalar.activation(k_endT[:, t, :], bank[2 + t][:], ACT.Copy).then_inc(kT_out, 1)
                for h in range(HEADS):
                    act.wait_ge(o_mm, l * HEADS + h + 1)
                    nc.scalar.activation(o_square(h), bank[h][:], ACT.Square).then_inc(o_sq, 1)
                for h in range(HEADS):
                    act.wait_ge(oss_mm, l * HEADS + h + 1)
                    nc.scalar.activation(att[:, h, :], bank[4 + h][:], ACT.Sqrt, bias=eps[:, 0:1],
                                         scale=1.0 / P).then_inc(o_root, 1)
                    if h >= 1:
                        round_head(h - 1)
                round_head(HEADS - 1)
                for i in range(CK):
                    act.wait_ge(centred, l * CK + i + 1)
                    nc.scalar.activation(glu[:, i, PAD:PAD + T], conv[:, i, :], ACT.Square).then_inc(c_sq, 1)
                act.wait_ge(var_mm, l + 1)
                nc.scalar.activation(q_fwd[:, 0, :], bank[5][:], ACT.Sqrt, bias=eps[:, 0:1],
                                     scale=1.0 / (CK * P)).then_inc(ln_root, 1)
                for i in range(CK):
                    act.wait_ge(ln_step, l * 5 + 2 + i)
                    nc.scalar.activation(conv[:, i, :], conv[:, i, :], ACT.Silu, bias=b_ln[:, i:i + 1],
                                         scale=g_ln[:, i:i + 1]).then_inc(c_act_done, 1)
                for i in range(CK):
                    act.wait_ge(c_act_done, l * CK + i + 1)
                    nc.scalar.activation(h_hi[:, i, :], conv[:, i, :], ACT.Copy).then_inc(y_round, 1)
                for p_ in range(PAIRS):
                    step(ZIN_UNITS + 2 * p_)
                    step(ZIN_UNITS + 2 * p_ + 1)
                    for t in range(2):
                        m = 2 * p_ + t
                        square(m, t, DK + l * 3 * DK + DK + m + 1, (n + 1) * DK + m - 1)

            act.wait_ge(const_ready, CONSTS)
            act.wait_ge(par_loaded, 48)
            nc.scalar.activation(c_act[:], c_act[:], ACT.Silu).then_inc(c_ready, 1)
            act.wait_ge(x_loaded, 16)
            for k in range(DK):
                if k >= 2:
                    act.wait_ge(ssq_ready, k - 1)
                nc.scalar.activation(tmp[:, k % 2, :], x[:, k, :], ACT.Square).then_inc(sq_ready, 1)
            for q in range(AHEAD):
                split(0, q, used=False)
            with act.Fori(0, LAYERS) as l:
                ffn(l, 0)
                mixer(l)
                ffn(l, 1)
            root(3 * LAYERS)
            act.wait_ge(gain_ready, 3 * LAYERS + 1)
            for k in range(DK):
                act.wait_ge(xn_ready, 3 * LAYERS * DK + k + 1)
                nc.scalar.activation(x[:, k, :], tmp[:, k % 3, :], ACT.Identity, bias=mod[:, 0, k:k + 1],
                                     scale=gain[:, k:k + 1]).then_inc(final_ready, 1)

        @block.vector
        def _(dve):
            def split(grp, q, tiles=KU):
                grp, slot = grp + q // AHEAD, q % AHEAD
                dve.wait_ge(w_round, grp * AHEAD + slot + 1)
                nc.vector.tensor_tensor(w_lo[:, slot, 0:tiles, :], raw[:, slot, 0:tiles, :],
                                        w_hi[:, slot, 0:tiles, :].bitcast(F32), ALU.subtract).then_inc(w_split, 1)

            def add_slice(blk, k):
                dve.wait_ge(ada_loaded[k % ADA_SLOTS], ((blk - ADA_PRE) * (DK // ADA_SLOTS) + k // ADA_SLOTS) * 16 + 16)
                src = ada_raw[:, k % ADA_SLOTS, :]
                if k == 0:
                    dve.wait_ge(ada_sum, blk)
                    nc.vector.tensor_scalar(ada_acc[:], src, c_act[:, k:k + 1], None, ALU.mult).then_inc(ada_mac, 1)
                else:
                    dve.wait_ge(ada_mac, (blk - ADA_PRE) * DK + k + ADA_SLOTS)
                    nc.vector.scalar_tensor_tensor(ada_acc[:], src, c_act[:, k:k + 1], ada_acc[:], ALU.mult,
                                                   ALU.add).then_inc(ada_mac, 1)

            def finish_ada(blk, into, at):
                dve.wait_ge(ada_sum, blk + 1)
                nc.vector.tensor_tensor(mod[:, bass.ds(at, 1), :].rearrange("p a k -> p (a k)"), bank[into][:, 0:DK],
                                        b_ada[:, bass.ds(blk, 1), :].rearrange("p a k -> p (a k)"), ALU.add).then_inc(mod_ready, 1)

            def inv_rms(n, scale_at, mods):
                dve.wait_ge(mod_ready, mods)
                nc.vector.scalar_tensor_tensor(gain[:], mod[:, scale_at, :], 1.0,
                                               g_norm[:, bass.ds(n, 1), :].rearrange("p a k -> p (a k)"), ALU.add,
                                               ALU.mult).then_inc(gain_ready, 1)
                dve.wait_ge(rms_root, n + 1)
                nc.vector.reciprocal(ssq[:], ssq[:]).then_inc(rms_step, 1)
                dve.wait_ge(rms_step, n + 1)

            def scale_x(n, k):
                nc.vector.tensor_tensor(tmp[:, k % 3, :], x[:, k, :], ssq[:], ALU.mult).then_inc(xn_ready, 1)

            def norm(n, scale_at, mods):
                inv_rms(n, scale_at, mods)
                for k in range(DK + 2):
                    if k < DK:
                        scale_x(n, k)
                    if k >= 2:
                        dve.wait_ge(h_round, n * DK + k - 1)
                        nc.vector.tensor_tensor(h_lo[:, k - 2, :], h_full[:, (k - 2) % 3, :], h_hi[:, k - 2, :].bitcast(F32),
                                                ALU.subtract).then_inc(h_ready, 1)

            def add_squares(slot, at, first=False):
                dve.wait_ge(sq_ready, at + 1)
                if not first:
                    dve.wait_ge(ssq_ready, at)
                nc.vector.tensor_tensor(ssq[:], ssq[:], tmp[:, slot, :], ALU.add).then_inc(ssq_ready, 1)

            def update(m, b, gate_col):
                xm = x[:, bass.ds(m, 1), :].rearrange("p k t -> p (k t)")
                nc.vector.scalar_tensor_tensor(xm, bank[b][:], gate_col, xm, ALU.mult, ALU.add).then_inc(x_ready, 1)

            def ffn(l, f):
                n = l * 3 + 2 * f
                grp = l * (LAYER_UNITS // AHEAD) + FFN_BASE[f] // AHEAD
                done = (l * 2 + f) * FK
                norm(n, 6 * f + 1, l * N_MOD + ADA_PRE + f * (ADA_IN + ADA_OUT))

                def in_block(b, blk, k0):
                    for m in range(4):
                        if m < 3:
                            split(grp + b, AHEAD + m)
                        if blk is not None:
                            add_slice(blk, k0 + m)
                    split(grp + b, AHEAD + 3)
                    for i in range(2):
                        dve.wait_ge(silu_done, done + 2 * b + i + 1)
                        nc.vector.tensor_tensor(tmp[:, i, :], tmp[:, i, :], bank[IN_UP[i]][:], ALU.mult).then_inc(g_ready, 1)
                    for i in range(2):
                        m = bass.ds(2 * b + i, 1)
                        dve.wait_ge(g_round, done + 2 * b + i + 1)
                        nc.vector.tensor_tensor(g_lo[:, m, :].rearrange("p k t -> p (k t)"), tmp[:, i, :],
                                                g_hi[:, m, :].rearrange("p k t -> p (k t)").bitcast(F32),
                                                ALU.subtract).then_inc(g_split, 1)

                in_block(0, None, 0)
                with dve.Fori(0, (BLOCKS - 1) // 2) as j:
                    blk = l * N_MOD + j + ADA_PRE
                    for i in range(2):
                        in_block(2 * j + 1 + i, blk if f == 0 else None, 4 * i)
                    if f == 0:
                        finish_ada(blk, ADA_BANK_IN, j + ADA_PRE)
                dve.wait_ge(mod_ready, l * N_MOD + ADA_PRE + ADA_IN + f * ADA_OUT)
                nc.vector.tensor_scalar(gate[:], mod[:, 2 + 6 * f, :], 0.5, None, ALU.mult).then_inc(gate_ready, 1)
                nc.vector.memset(ssq[:], 0.0).then_inc(gate_ready, 1)
                with dve.Fori(0, PAIRS // 2) as j:
                    blk = l * N_MOD + j + ADA_PRE + ADA_IN + f * ADA_OUT
                    for i in range(2):
                        for m in range(OUT_UNITS):
                            q = i * OUT_UNITS + m + AHEAD
                            tiles = FK % KU if q % OUT_UNITS == OUT_UNITS - 1 else KU
                            split(grp + BLOCKS + j * (2 * OUT_UNITS // AHEAD), q, tiles)
                            if m < 4:
                                add_slice(blk, 4 * i + m)
                        dve.wait_ge(gate_ready, l * 5 + 3 * f + 2)
                        for t in range(2):
                            m = 4 * j + 2 * i + t
                            update(m, (OUT_A, OUT_B)[i][t], gate[:, bass.ds(m, 1)])
                        for t in range(2):
                            add_squares(t, (n + 1) * DK + 4 * j + 2 * i + t)
                    finish_ada(blk, ADA_BANK_OUT, j + (ADA_PRE + ADA_IN if f == 0 else 0))

            def mixer(l):
                n = l * 3 + 1
                grp = l * (LAYER_UNITS // AHEAD) + MIX_BASE // AHEAD

                def step(u):
                    split(grp, u + AHEAD)

                taps = [0]

                def conv_taps(tiles, first, last):
                    for j in range(first, last):
                        for i in tiles:
                            win = glu[:, i, j:j + T]
                            if j == 0:
                                ins = nc.vector.tensor_scalar(conv[:, i, :], win, w_dw[:, i, 0:1], b_dw[:, i:i + 1], ALU.mult, ALU.add)
                            else:
                                dve.wait_ge(tap_done, l * TAPS * CK + taps[0] - 1)
                                ins = nc.vector.scalar_tensor_tensor(conv[:, i, :], win, w_dw[:, i, j:j + 1], conv[:, i, :],
                                                                     ALU.mult, ALU.add)
                            ins.then_inc(tap_done, 1)
                            taps[0] += 1

                norm(n, 4, l * N_MOD + ADA_PRE + ADA_IN + ADA_OUT)
                step(0)
                step(1)
                dve.wait_ge(glrw_round, l + 1)
                nc.vector.tensor_tensor(glr_lo[:], glr_raw[:], glr_hi[:].bitcast(F32), ALU.subtract).then_inc(glrw_split, 1)
                step(2)
                step(3)
                for i in range(2):
                    dve.wait_ge(sig_done, l * CK + i + 1)
                    nc.vector.tensor_tensor(glu[:, i, PAD:PAD + T], tmp[:, i, :], bank[i][:], ALU.mult).then_inc(glu_done, 1)
                dve.wait_ge(built, l * BUILDS + BUILDS)
                dve.wait_ge(glu_done, l * CK + 2)
                for u in range(4, 8):
                    step(u)
                    if u < 7:
                        conv_taps((0, 1), 3 * (u - 4), 3 * (u - 3))
                for i in range(2):
                    dve.wait_ge(sig_done, l * CK + 2 + i + 1)
                    nc.vector.tensor_tensor(glu[:, 2 + i, PAD:PAD + T], tmp[:, i, :], bank[4 + i][:], ALU.mult).then_inc(glu_done, 1)
                conv_taps((0, 1), 9, 12)
                step(8)
                conv_taps((0, 1), 12, 15)
                step(9)
                for t in range(2):
                    dve.wait_ge(soft, l * 8 + 7 + t)
                    nc.vector.scalar_tensor_tensor(q_fwd[:, t, :], k_fwd[:, t, :], 0.0, k_bwd[:, t, :], ALU.min,
                                                   ALU.subtract).then_inc(logsig, 1)
                for t in range(2):
                    dve.wait_ge(logsig, l * 2 + t + 1)
                    nc.vector.tensor_tensor_scan(bc[:, t, :], restart[:], q_fwd[:, t, :], 0.0, ALU.mult, ALU.add).then_inc(scanned, 1)
                for t in range(2):
                    dve.wait_ge(scanned, l * 2 + t + 1)
                    b3 = bc[:, t, :].rearrange("p (c j) -> p c j", j=CHUNK)
                    nc.vector.tensor_tensor(k_end[:, t, :].rearrange("p (c j) -> p c j", j=CHUNK),
                                            b3[:, :, CHUNK - 1:CHUNK].to_broadcast([P, NCHUNK, CHUNK]), b3,
                                            ALU.subtract).then_inc(diff, 1)
                step(10)
                conv_taps((0, 1), 15, 18)
                dve.wait_ge(exps, l * 8 + 8)
                for t in range(2):
                    for out, ex in ((q_fwd, k_bwd), (q_bwd, k_fwd)):
                        nc.vector.scalar_tensor_tensor(out[:, t, :], bank[2 + t][:], CHUNK ** -0.5, ex[:, t, :], ALU.mult,
                                                       ALU.mult).then_inc(qk_done, 1)
                step(11)
                for t in range(2):
                    for ex in (k_bwd, k_fwd, k_end):
                        nc.vector.tensor_tensor(ex[:, t, :], ex[:, t, :], bank[4 + t][:], ALU.mult).then_inc(qk_done, 1)
                for u in range(12, 16):
                    step(u)
                    conv_taps((0, 1), 18 + 3 * (u - 12), 21 + 3 * (u - 12))
                step(16)
                conv_taps((0, 1), 30, 31)
                conv_taps((2, 3), 0, 2)
                step(17)
                conv_taps((2, 3), 2, 5)

                def select(heads, done, tap):
                    dve.wait_ge(att_mm, l * HEADS + heads[1] + 1)
                    conv_taps((2, 3), tap, tap + 1)
                    for mask, banks in ((mask_f, (6, 0)), (mask_b, (7, 1))):
                        if mask is mask_b:
                            dve.wait_ge(att_sel, l * 8 + done + 2)
                            conv_taps((2, 3), tap + 1, tap + 2)
                        for h, b in zip(heads, banks):
                            where = mask[:].bitcast(U32).rearrange("p (o i) -> p o i", o=1).to_broadcast([P, TB, P])
                            nc.vector.copy_predicated(att[:, h, :].rearrange("p (b i) -> p b i", i=P), where,
                                                      bank[b][:].rearrange("p (b i) -> p b i", i=P)).then_inc(att_sel, 1)

                select((0, 1), 0, 5)
                step(18)
                step(19)
                select((2, 3), 4, 7)
                conv_taps((2, 3), 9, 16)
                for t in range(2):
                    ev, od = (4, 5) if t == 0 else (6, 7)
                    dve.wait_ge(u_mm, l * 2 + t + 1)
                    for c in range(NCHUNK - 1):
                        u = bank[od if c % 2 else ev][:, (c // 2) * P:(c // 2 + 1) * P]
                        if c == 0:
                            ins = nc.vector.tensor_copy(state[:, t, 0, :], u)
                        else:
                            dve.wait_ge(st, (l * 2 + t) * (NCHUNK - 1) + c)
                            ins = nc.vector.scalar_tensor_tensor(state[:, t, c, :], state[:, t, c - 1, :], end_exp[:, t, c:c + 1],
                                                                 u, ALU.mult, ALU.add)
                        ins.then_inc(st, 1)
                conv_taps((2, 3), 16, 31)
                for h in range(HEADS):
                    inv, y = att[:, h, :], v[:, h, :]
                    dve.wait_ge(o_sq, l * HEADS + h + 1)
                    nc.vector.scalar_tensor_tensor(y, bank[h][:], g_gla[:, h:h + 1], r_act[:, h, :], ALU.mult,
                                                   ALU.mult).then_inc(o_norm, 1)
                    dve.wait_ge(o_root, l * HEADS + h + 1)
                    nc.vector.reciprocal(inv, inv).then_inc(o_norm, 1)
                    dve.wait_ge(o_norm, l * 12 + 3 * h + 2)
                    nc.vector.tensor_tensor(y, y, inv, ALU.mult).then_inc(o_norm, 1)
                    if h >= 1:
                        head_lo(l, h - 1)
                head_lo(l, HEADS - 1)
                dve.wait_ge(mean_mm, l + 1)
                for i in range(CK):
                    nc.vector.scalar_tensor_tensor(conv[:, i, :], bank[4][:], -1.0 / (CK * P), conv[:, i, :], ALU.mult,
                                                   ALU.add).then_inc(centred, 1)
                inv = q_fwd[:, 0, :]
                dve.wait_ge(ln_root, l + 1)
                nc.vector.reciprocal(inv, inv).then_inc(ln_step, 1)
                dve.wait_ge(ln_step, l * 5 + 1)
                for i in range(CK):
                    nc.vector.tensor_tensor(conv[:, i, :], conv[:, i, :], inv, ALU.mult).then_inc(ln_step, 1)
                nc.vector.memset(ssq[:], 0.0).then_inc(gate_ready, 1)
                for i in range(CK):
                    dve.wait_ge(y_round, l * DK + HEADS + i + 1)
                    nc.vector.tensor_tensor(h_lo[:, i, :], conv[:, i, :], h_hi[:, i, :].bitcast(F32), ALU.subtract).then_inc(y_ready, 1)
                dve.wait_ge(gate_ready, l * 5 + 3)
                for p_ in range(PAIRS):
                    step(ZIN_UNITS + 2 * p_)
                    step(ZIN_UNITS + 2 * p_ + 1)
                    for t in range(2):
                        m = 2 * p_ + t
                        update(m, m, mod[:, 5, m:m + 1])
                    for t in range(2):
                        add_squares(t, (n + 1) * DK + 2 * p_ + t)

            def head_lo(l, h):
                dve.wait_ge(y_round, l * DK + h + 1)
                nc.vector.tensor_tensor(h_lo[:, CK + h, :], v[:, h, :], h_hi[:, CK + h, :].bitcast(F32),
                                        ALU.subtract).then_inc(y_ready, 1)

            nc.vector.memset(ssq[:], 0.0).then_inc(w_split, AHEAD)
            nc.vector.memset(gain[:, 0:1], 0.0).then_inc(ada_mac, ADA_SLOTS)
            nc.vector.memset(gain[:, 1:2], 0.0).then_inc(x_ready, DK)
            dve.wait_ge(w_split, AHEAD)
            for k in range(DK):
                add_squares(k % 2, k, first=k == 0)
            for q in range(AHEAD):
                split(0, q)
            dve.wait_ge(c_ready, 1)
            for b in range(ADA_PRE):
                for k in range(DK):
                    dve.wait_ge(pre_loaded[b * DK + k], 16)
                    if k == 0:
                        if b:
                            dve.wait_ge(ada_sum, b)
                        nc.vector.tensor_scalar(ada_acc[:], pre[:, b, k, :], c_act[:, k:k + 1], None, ALU.mult).then_inc(pre_mac, 1)
                    else:
                        dve.wait_ge(pre_mac, b * DK + k)
                        nc.vector.scalar_tensor_tensor(ada_acc[:], pre[:, b, k, :], c_act[:, k:k + 1], ada_acc[:], ALU.mult,
                                                       ALU.add).then_inc(pre_mac, 1)
                finish_ada(b, ADA_BANK_IN, b)
            with dve.Fori(0, LAYERS) as l:
                ffn(l, 0)
                mixer(l)
                ffn(l, 1)
            inv_rms(3 * LAYERS, 1, LAYERS * N_MOD + ADA_PRE)
            for k in range(DK):
                if k >= 3:
                    dve.wait_ge(final_ready, k - 2)
                scale_x(3 * LAYERS, k)


def kernel(**inputs):
    import numpy as np
    import concourse.bacc as bacc
    from concourse import mybir as mb
    from concourse.bass_utils import run_bass_kernel_spmd

    a = {n: np.asarray(v) for n, v in inputs.items()}
    L = LAYERS

    def columns(z):
        z = z.reshape(*z.shape[:-1], -1, P)
        return np.moveaxis(z, -1, 0)

    laid = {
        "xT": a["x"][0].T,
        "cT": columns(a["c"][0]),
        "w_ada": np.concatenate([*a["w_ada"], a["w_ada_final"]], axis=1),
        "b_adaT": columns(np.concatenate([a["b_ada"].reshape(-1), a["b_ada_final"]]).reshape(-1, D)),
        "g_normT": columns(np.stack([z for l in range(L) for z in (a["g_norm_ffn1"][l], a["g_norm_mix"][l], a["g_norm_ffn2"][l])]
                                    + [a["g_norm_final"]])),
        "w_ffn1_in": a["w_ffn1_in"], "w_ffn1_out": a["w_ffn1_out"], "w_in": a["w_in"],
        "w_glr": np.moveaxis(a["w_in"][:, :, GLR_COL:].reshape(L * DK, P, RANK), 1, 0),
        "w_ffn2_in": a["w_ffn2_in"], "w_ffn2_out": a["w_ffn2_out"], "w_out": a["w_out"],
        "w_dwT": np.moveaxis(columns(a["w_dw"]), 2, 3),
        "mix_colsT": np.concatenate([columns(a[n]) for n in ("b_dw", "g_conv_ln", "b_conv_ln", "b_gate")]
                                    + [columns(a["g_gla_norm"].reshape(L, -1))], axis=2),
        "w_gate_up": np.moveaxis(a["w_gate_up"], 1, 0),
    }
    nc = bacc.Bacc("TRN2", target_bir_lowering=False, num_devices=1)
    arrays, args = {}, []
    for name, z in laid.items():
        z = np.ascontiguousarray(z)
        arrays[f"in_{name}"] = z
        args.append(nc.dram_tensor(f"in_{name}", z.shape, mb.dt.from_np(z.dtype), kind="ExternalInput").ap())
    args.append(nc.dram_tensor("out_T", (D, T), F32, kind="ExternalOutput").ap())
    trunk(nc, *args)
    r = run_bass_kernel_spmd(nc, [arrays], core_ids=[0])
    return np.ascontiguousarray(r.results[0]["out_T"].T)[None]
```

```python
from contextlib import ExitStack

import concourse.bass as bass
from concourse import mybir

F32 = mybir.dt.float32
F32R = mybir.dt.float32r
U32 = mybir.dt.uint32
ALU = mybir.AluOpType
ACT = mybir.ActivationFunctionType

P = 128
LAYERS = 2
D = 1024
T = 512
DK = D // P
D_FF = 2816
FK = D_FF // P
N_MOD = 9
EPS = 1e-6
HEADS = 4
CHUNK = 64
NCHUNK = T // CHUNK
TB = T // P
TAPS = 31
CK = 4
RANK = 16
TAU = 16.0
D_IN = 2576

KU, CU = 4, 256
AHEAD = 4
BLOCKS = D_FF // CU
PAIRS = D // CU
OUT_UNITS = -(-FK // KU)
IN_UNITS = 4 * BLOCKS
FFN_UNITS = IN_UNITS + PAIRS * OUT_UNITS
ZIN_UNITS = 20
MIX_UNITS = ZIN_UNITS + 2 * PAIRS
LAYER_UNITS = 2 * FFN_UNITS + MIX_UNITS
FFN_BASE = (0, FFN_UNITS + MIX_UNITS)
MIX_BASE = FFN_UNITS
ZIN_COLS = (0, 512, 256, 768, 1024, 1280, 1536, 1792, 2048, 2304)
GLR_COL = 2560
assert IN_UNITS % AHEAD == 0 and (PAIRS * OUT_UNITS) % AHEAD == 0 and MIX_UNITS % AHEAD == 0
assert BLOCKS % 2 == 1 and OUT_UNITS * 2 % AHEAD == 0

MIX_OUT = ((0, 0), (1, 0), (0, 1), (1, 1), (2, 0), (2, 1), (3, 0), (3, 1))

ADA_PRE = 2
ADA_SLOTS = 2
ADA_IN = (BLOCKS - 1) // 2
ADA_OUT = PAIRS // 2
assert ADA_IN + 2 * ADA_OUT == N_MOD


def trunk(nc, xT, cT, w_ada, b_adaT, g_normT, w_ffn1_in, w_ffn1_out, w_in, w_glr, w_ffn2_in, w_ffn2_out, w_out,
          w_dwT, mix_colsT, w_gate_up, outT):
    ffn_in = [w.rearrange("l (c k p) n -> p (l c) k n", p=P, k=KU) for w in (w_ffn1_in, w_ffn2_in)]
    ffn_out = [w.rearrange("l (k p) n -> p (l k) n", p=P) for w in (w_ffn1_out, w_ffn2_out)]
    z_in = w_in.rearrange("l (c k p) n -> p (l c) k n", p=P, k=KU)
    y_out = w_out.rearrange("l (c k p) n -> p (l c) k n", p=P, k=KU)
    ada = w_ada.rearrange("(k p) n -> p k n", p=P)

    with ExitStack() as ctx:
        def sem(name):
            return ctx.enter_context(nc.semaphore(name))

        top = [-(-nc.sbuf_base // 64) * 64]

        def place(name, shape, dt=F32, at=None):
            size = 1
            for n in shape[1:]:
                size *= n
            size *= 4
            off = top[0] if at is None else at[0]
            (top if at is None else at)[0] = off + -(-size // 32) * 32
            return nc.alloc_sbuf_tensor_at(name, shape, dt, offset=off)

        x = place("x", [P, DK, T])
        h_hi = place("h_hi", [P, DK, T], F32R)
        h_lo = place("h_lo", [P, DK, T], F32R)
        raw = place("raw", [P, AHEAD, KU, CU])
        w_hi = place("w_hi", [P, AHEAD, KU, CU], F32R)
        w_lo = place("w_lo", [P, AHEAD, KU, CU], F32R)
        ada_raw = place("ada_raw", [P, ADA_SLOTS, D])
        ada_acc = place("ada_acc", [P, D])
        tmp = place("tmp", [P, 3, T])
        ssq = place("ssq", [P, T])
        inv = place("inv", [P, TB])
        ones = place("ones", [P, P])
        eps = place("eps", [P, 1])
        ident = place("ident", [P, P])
        mask_f = place("mask_f", [P, P])
        mask_b = place("mask_b", [P, P])
        mod = place("mod", [P, N_MOD, DK])
        b_ada = place("b_ada", [P, LAYERS * N_MOD + 2, DK])
        g_norm = place("g_norm", [P, 3 * LAYERS + 1, DK])
        gain = place("gain", [P, DK])
        gate = place("gate", [P, DK])
        c_act = place("c_act", [P, DK])
        shared = top[0]
        ffn_map = [shared]
        g_hi = place("g_hi", [P, FK, T], F32R, ffn_map)
        g_lo = place("g_lo", [P, FK, T], F32R, ffn_map)
        pre_map = [shared]
        pre = place("pre", [P, ADA_PRE, DK, D], F32, pre_map)
        mix_map = [shared]
        PAD = TAPS - 1
        glu = place("glu", [P, CK, PAD + T], F32, mix_map)
        conv = place("conv", [P, CK, T], F32, mix_map)
        bc = place("bc", [P, 2, T], F32, mix_map)
        k_bwd = place("k_bwd", [P, 2, T], F32, mix_map)
        k_fwd = place("k_fwd", [P, 2, T], F32, mix_map)
        k_end = place("k_end", [P, 2, T], F32, mix_map)
        q_fwd = place("q_fwd", [P, 2, T], F32, mix_map)
        q_bwd = place("q_bwd", [P, 2, T], F32, mix_map)
        v = place("v", [P, TB, HEADS * P], F32, mix_map)
        att = place("att", [P, HEADS, T], F32, mix_map)
        k_endT = place("k_endT", [P, 2, T], F32, mix_map)
        prod = place("prod", [P, 3, T], F32, [mix_map[0]])
        state = place("state", [P, 2, NCHUNK - 1, P], F32, mix_map)
        r_act = place("r_act", [P, HEADS, T], F32, mix_map)
        inv_o = place("inv_o", [P, HEADS, TB], F32, mix_map)
        end_exp = place("end_exp", [P, 2, NCHUNK], F32, mix_map)
        w_dw = place("w_dw", [P, CK, TAPS], F32, mix_map)
        cols = place("cols", [P, 18], F32, mix_map)
        glr_raw = place("glr_raw", [P, DK, RANK], F32, mix_map)
        glr_hi = place("glr_hi", [P, DK, RANK], F32R, mix_map)
        glr_lo = place("glr_lo", [P, DK, RANK], F32R, mix_map)
        glr = place("glr", [RANK, T], F32, mix_map)
        up_w = place("up_w", [RANK, 2 * P], F32, mix_map)
        restart = place("restart", [P, T], F32, mix_map)
        assert max(ffn_map[0], pre_map[0], mix_map[0]) <= nc.sbuf_usable_end, (ffn_map, pre_map, mix_map)
        b_dw, g_ln, b_ln, b_gate, g_gla = (cols[:, a:b] for a, b in ((0, 4), (4, 8), (8, 12), (12, 14), (14, 18)))

        bank = [ctx.enter_context(nc.psum_tensor(f"bank{i}", [P, T], F32)) for i in range(8)]
        IN_GATE, IN_UP, OUT_A, OUT_B = (0, 1), (2, 3), (4, 5), (6, 7)
        ADA_BANK_IN, ADA_BANK_OUT, STAT, SPREAD = 6, 2, 1, 7

        w_loaded = [sem(f"w_loaded{s}") for s in range(AHEAD)]
        w_round = sem("w_round")
        w_split = sem("w_split")
        w_used = sem("w_used")
        even_done = sem("even_done")
        par_loaded = sem("par_loaded")
        pre_loaded = [sem(f"pre_loaded{b}") for b in range(ADA_PRE * DK)]
        x_loaded = sem("x_loaded")
        mixp_loaded = sem("mixp_loaded")
        ada_loaded = [sem(f"ada_loaded{s}") for s in range(ADA_SLOTS)]
        ada_mac = sem("ada_mac")
        ada_sum = sem("ada_sum")
        mod_ready = sem("mod_ready")
        pre_mac = sem("pre_mac")
        c_ready = sem("c_ready")
        const_ready = sem("const_ready")
        x_ready = sem("x_ready")
        sq_ready = sem("sq_ready")
        ssq_ready = sem("ssq_ready")
        stat_ready = sem("stat_ready")
        rms_root = sem("rms_root")
        rms_step = sem("rms_step")
        spread = sem("spread")
        gain_ready = sem("gain_ready")
        xn_ready = sem("xn_ready")
        h_round = sem("h_round")
        h_ready = sem("h_ready")
        silu_done = sem("silu_done")
        g_ready = sem("g_ready")
        g_round = sem("g_round")
        g_split = sem("g_split")
        gate_ready = sem("gate_ready")
        final_ready = sem("final_ready")
        stored = sem("stored")
        built = sem("built")
        sig_done = sem("sig_done")
        glu_done = sem("glu_done")
        tap_done = sem("tap_done")
        prod_ready = sem("prod_ready")
        pool_tap = sem("pool_tap")
        glrw_round = sem("glrw_round")
        glrw_split = sem("glrw_split")
        glr_done = sem("glr_done")
        glr_out = sem("glr_out")
        z_done = sem("z_done")
        soft = sem("soft")
        logsig = sem("logsig")
        scanned = sem("scanned")
        diff = sem("diff")
        exps = sem("exps")
        qk_done = sem("qk_done")
        v_out = sem("v_out")
        r_out = sem("r_out")
        att_mm = sem("att_mm")
        att_sel = sem("att_sel")
        kT_mm = sem("kT_mm")
        kT_out = sem("kT_out")
        u_mm = sem("u_mm")
        st = sem("st")
        o_mm = sem("o_mm")
        o_sq = sem("o_sq")
        o_gated = sem("o_gated")
        oss_mm = sem("oss_mm")
        o_root = sem("o_root")
        o_inv = sem("o_inv")
        o_diag = sem("o_diag")
        o_spread = sem("o_spread")
        o_norm = sem("o_norm")
        y_round = sem("y_round")
        y_ready = sem("y_ready")
        mean_mm = sem("mean_mm")
        centred = sem("centred")
        c_sq = sem("c_sq")
        var_mm = sem("var_mm")
        ln_root = sem("ln_root")
        ln_inv = sem("ln_inv")
        ln_spread = sem("ln_spread")
        ln_done = sem("ln_done")
        c_act_done = sem("c_act_done")

        BUILDS = 4
        CONSTS = 11

        def o_square(h):
            return (q_bwd if h < 2 else k_fwd)[:, h % 2, :]

        block = ctx.enter_context(nc.Block())

        @block.sync
        def _(sp):
            sp.dma_start(c_act[:], cT).then_inc(par_loaded, 16)
            sp.dma_start(b_ada[:], b_adaT).then_inc(par_loaded, 16)
            sp.dma_start(g_norm[:], g_normT).then_inc(par_loaded, 16)
            sp.dma_start(x[:], xT.rearrange("(k p) t -> p k t", p=P)).then_inc(x_loaded, 16)
            for b in range(ADA_PRE):
                for k in range(DK):
                    sp.dma_start(pre[:, b, k, :], ada[:, k, b * D:(b + 1) * D]).then_inc(pre_loaded[b * DK + k], 16)

            def load(unit, slot, src, tiles=KU):
                sp.wait_ge(w_split, unit + 1)
                sp.dma_start(raw[:, slot, 0:tiles, :], src).then_inc(w_loaded[slot], 16)

            def load_block(l, f, base, b, s):
                for half in range(2):
                    for c in range(2):
                        load(base + 4 * b + 2 * half + c, (s + 2 * half + c) % AHEAD,
                             ffn_in[f][:, 2 * l + c, :, bass.ds(b * CU + half * D_FF, CU)])

            def load_ffn(l, f):
                base = l * LAYER_UNITS + FFN_BASE[f]
                load_block(l, f, base, 0, 0)
                with sp.Fori(0, (BLOCKS - 1) // 2) as j:
                    for i in range(2):
                        load_block(l, f, base, 2 * j + 1 + i, 0)
                with sp.Fori(0, PAIRS // 2) as j:
                    for i in range(2):
                        for n in range(OUT_UNITS):
                            tiles = min(KU, FK - n * KU)
                            q = i * OUT_UNITS + n
                            load(base + IN_UNITS + j * 2 * OUT_UNITS + q, q % AHEAD,
                                 ffn_out[f][:, bass.ds(l * FK + n * KU, tiles), bass.ds((2 * j + i) * CU, CU)], tiles)

            with sp.Fori(0, LAYERS) as l:
                load_ffn(l, 0)
                base = l * LAYER_UNITS + MIX_BASE
                for n, col in enumerate(ZIN_COLS):
                    for c in range(2):
                        load(base + 2 * n + c, (2 * n + c) % AHEAD, z_in[:, 2 * l + c, :, col:col + CU])
                for n, (p_, c) in enumerate(MIX_OUT):
                    load(base + ZIN_UNITS + n, n % AHEAD, y_out[:, 2 * l + c, :, p_ * CU:(p_ + 1) * CU])
                load_ffn(l, 1)
            load_block(0, 0, LAYERS * LAYER_UNITS, 0, 0)
            for k in range(DK):
                sp.wait_ge(final_ready, k + 1)
                sp.dma_start(outT[k * P:(k + 1) * P, :], x[:, k, :]).then_inc(stored, 16)
            sp.wait_ge(stored, 16 * DK)

        @block.gpsimd
        def _(pool):
            def load_ada(blk):
                for k in range(DK):
                    pool.wait_ge(ada_mac, (blk - ADA_PRE) * DK + k + 1)
                    pool.dma_start(ada_raw[:, k % ADA_SLOTS, :],
                                   ada[:, k, bass.ds(blk * D, D)]).then_inc(ada_loaded[k % ADA_SLOTS], 16)

            pool.memset(eps[:], EPS).then_inc(const_ready, 1)
            pool.memset(ones[:], 1.0).then_inc(const_ready, 1)
            pool.memset(mask_f[:], 1.0).then_inc(const_ready, 1)
            pool.memset(mask_b[:], 1.0).then_inc(const_ready, 1)
            pool.memset(ident[:], 0.0).then_inc(const_ready, 1)
            pool.wait_ge(const_ready, 5)
            pool.affine_select(out=ident[:], in_=ident[:], compare_op=ALU.not_equal, fill=1.0, base=0,
                               pattern=[[-1, P]], channel_multiplier=1).then_inc(const_ready, 1)
            pool.affine_select(out=mask_f[:], in_=mask_f[:], compare_op=ALU.is_ge, fill=0.0, base=0,
                               pattern=[[1, P]], channel_multiplier=-1).then_inc(const_ready, 1)
            pool.affine_select(out=mask_b[:], in_=mask_b[:], compare_op=ALU.is_ge, fill=0.0, base=-1,
                               pattern=[[-1, P]], channel_multiplier=1).then_inc(const_ready, 1)
            pool.wait_ge(const_ready, 8)
            pool.memset(mask_f[0:CHUNK, CHUNK:P], 0.0).then_inc(const_ready, 1)
            pool.memset(mask_b[CHUNK:P, 0:CHUNK], 0.0).then_inc(const_ready, 1)
            pool.memset(mask_b[0:CHUNK, CHUNK:P], 0.0).then_inc(const_ready, 1)
            with pool.Fori(0, LAYERS) as l:
                with pool.Fori(0, ADA_IN) as j:
                    load_ada(l * N_MOD + j + ADA_PRE)
                with pool.Fori(0, ADA_OUT) as j:
                    load_ada(l * N_MOD + j + (ADA_PRE + ADA_IN))
                pool.wait_ge(w_used, l * LAYER_UNITS + MIX_BASE)
                pool.dma_start(w_dw[:], w_dwT[:, bass.ds(l, 1), :, :].rearrange("p l c t -> p (l c) t")).then_inc(mixp_loaded, 16)
                pool.dma_start(cols[:], mix_colsT[:, bass.ds(l, 1), :].rearrange("p l c -> p (l c)")).then_inc(mixp_loaded, 16)
                pool.dma_start(glr_raw[:], w_glr[:, bass.ds(l * DK, DK), :]).then_inc(mixp_loaded, 16)
                pool.dma_start(up_w[:], w_gate_up[:, bass.ds(l, 1), :].rearrange("r l c -> r (l c)")).then_inc(mixp_loaded, 16)
                pool.memset(glu[:, :, 0:PAD], 0.0).then_inc(built, 1)
                pool.memset(att[:], 0.0).then_inc(built, 1)
                by_chunk = restart[:].rearrange("p (c j) -> p c j", j=CHUNK)
                pool.memset(by_chunk[:, :, 0:1], 0.0).then_inc(built, 1)
                pool.memset(by_chunk[:, :, 1:CHUNK], 1.0).then_inc(built, 1)
                for s, i in enumerate((1, 3)):
                    for j in range(1, TAPS):
                        a = s * (TAPS - 1) + j - 1
                        pool.wait_ge(prod_ready, l * 2 * TAPS + s * TAPS + j + 1)
                        if a:
                            pool.wait_ge(pool_tap, l * 2 * (TAPS - 1) + a)
                        pool.tensor_tensor(conv[:, i, :], conv[:, i, :], prod[:, a % 3, :], ALU.add).then_inc(pool_tap, 1)
                with pool.Fori(0, ADA_OUT) as j:
                    load_ada(l * N_MOD + j + (ADA_PRE + ADA_IN + ADA_OUT))

        @block.tensor
        def _(pe):
            def three(out, a_hi, a_lo, b_hi, b_lo, first, last):
                nc.tensor.matmul(out, a_hi, b_hi, start=first, stop=False)
                nc.tensor.matmul(out, a_hi, b_lo, start=False, stop=False)
                return nc.tensor.matmul(out, a_lo, b_hi, start=False, stop=last)

            def unit(u, slot, banks, rhs_hi, rhs_lo, k0, total):
                pe.wait_ge(w_split, u + 1 + AHEAD)
                for k in range(KU):
                    for m in range(2):
                        mm = three(bank[banks[m]][:], w_hi[:, slot, k, m * P:(m + 1) * P], w_lo[:, slot, k, m * P:(m + 1) * P],
                                   rhs_hi[:, k0 + k, :], rhs_lo[:, k0 + k, :], k0 + k == 0, k0 + k == total - 1)
                mm.then_inc(w_used, 1)

            def unit_as_ready(u, slot, banks, rhs_hi, rhs_lo, k0, total, rounded, split, at, tiles=KU,
                              ends_pair=False):
                pe.wait_ge(w_split, u + 1 + AHEAD)
                for k in range(tiles):
                    first, last = k0 + k == 0, k0 + k == total - 1
                    w = [(w_hi[:, slot, k, m * P:(m + 1) * P], w_lo[:, slot, k, m * P:(m + 1) * P]) for m in range(2)]
                    pe.wait_ge(rounded, at + k + 1)
                    for m in range(2):
                        nc.tensor.matmul(bank[banks[m]][:], w[m][0], rhs_hi[:, k0 + k, :], start=first, stop=False)
                        nc.tensor.matmul(bank[banks[m]][:], w[m][1], rhs_hi[:, k0 + k, :], start=False, stop=False)
                    pe.wait_ge(split, at + k + 1)
                    for m in range(2):
                        mm = nc.tensor.matmul(bank[banks[m]][:], w[m][0], rhs_lo[:, k0 + k, :], start=False, stop=last)
                        if ends_pair and k == tiles - 1 and m == 0:
                            mm.then_inc(even_done, 1)
                mm.then_inc(w_used, 1)

            def unit_by_tile(u, slot, banks, rhs_hi, rhs_lo, k0, tiles=KU):
                pe.wait_ge(w_split, u + 1 + AHEAD)
                for m in range(2):
                    for k in range(tiles):
                        mm = three(bank[banks[m]][:], w_hi[:, slot, k, m * P:(m + 1) * P], w_lo[:, slot, k, m * P:(m + 1) * P],
                                   rhs_hi[:, k0 + k, :], rhs_lo[:, k0 + k, :], False, k == tiles - 1)
                    if m == 0:
                        mm.then_inc(even_done, 1)
                mm.then_inc(w_used, 1)

            def ada_flush(blk, into):
                pe.wait_ge(ada_mac, (blk - ADA_PRE + 1) * DK + ADA_SLOTS)
                pe.wait_ge(mod_ready, blk)
                for n in range(DK):
                    mm = nc.tensor.matmul(bank[into][:, n:n + 1], ada_acc[:, n * P:(n + 1) * P], ones[:, 0:1],
                                          start=True, stop=True)
                mm.then_inc(ada_sum, 1)

            def column_sums(into, col, src, first, last):
                for b in range(TB):
                    mm = nc.tensor.matmul(bank[into][:, col + b:col + b + 1], src[:, b * P:(b + 1) * P], ones[:, 0:1],
                                          start=first and b == 0, stop=last, skip_group_check=True)
                return mm

            def stat(n):
                pe.wait_ge(ssq_ready, (n + 1) * DK)
                column_sums(STAT, 0, ssq, True, False)
                pe.wait_ge(sq_ready, (n + 1) * DK)
                column_sums(STAT, 0, tmp[:, 1, :], False, True).then_inc(stat_ready, 1)
                pe.wait_ge(rms_step, 2 * n + 2)
                nc.tensor.matmul(bank[SPREAD][:], ones[:], ssq[:], start=True, stop=True).then_inc(spread, 1)

            def ffn(l, f):
                n = l * 3 + 2 * f
                base = l * LAYER_UNITS + FFN_BASE[f]
                done = (l * 2 + f) * FK
                stat(n)

                def in_block(b, first):
                    if not first:
                        pe.wait_ge(silu_done, done + 2 * b)
                    for c in range(2):
                        if first:
                            unit_as_ready(base + c, c, IN_GATE, h_hi, h_lo, c * KU, DK, h_round, h_ready, n * DK + c * KU)
                        else:
                            unit(base + 4 * b + c, c, IN_GATE, h_hi, h_lo, c * KU, DK)
                    if not first:
                        pe.wait_ge(g_ready, done + 2 * b)
                    for c in range(2):
                        unit(base + 4 * b + 2 + c, 2 + c, IN_UP, h_hi, h_lo, c * KU, DK)

                in_block(0, True)
                with pe.Fori(0, (BLOCKS - 1) // 2) as j:
                    for i in range(2):
                        in_block(2 * j + 1 + i, False)
                    if f == 0:
                        ada_flush(l * N_MOD + j + ADA_PRE, ADA_BANK_IN)
                with pe.Fori(0, PAIRS // 2) as j:
                    for i in range(2):
                        banks = (OUT_A, OUT_B)[i]
                        pe.wait_ge(x_ready, l * 3 * DK + 2 * f * DK + 4 * j + 2 * i + DK - 2)
                        if i == 1:
                            pe.wait_ge(mod_ready, l * N_MOD + ADA_PRE + ADA_IN + f * ADA_OUT)
                        for m in range(OUT_UNITS):
                            q = i * OUT_UNITS + m
                            u, slot = base + IN_UNITS + j * 2 * OUT_UNITS + q, q % AHEAD
                            if i == 0:
                                pe.wait_ge(g_split, done + min(m * KU + KU, FK))
                            if m == OUT_UNITS - 1:
                                unit_by_tile(u, slot, banks, g_hi, g_lo, m * KU, FK - m * KU)
                            else:
                                unit(u, slot, banks, g_hi, g_lo, m * KU, FK)
                    ada_flush(l * N_MOD + j + ADA_PRE + ADA_IN + f * ADA_OUT, ADA_BANK_OUT)

            def mixer(l):
                n = l * 3 + 1
                base = l * LAYER_UNITS + MIX_BASE
                stat(n)
                for c in range(2):
                    unit_as_ready(base + c, c, (0, 1), h_hi, h_lo, c * KU, DK, h_round, h_ready, n * DK + c * KU)
                for i in range(1, 4):
                    for c in range(2):
                        unit(base + 2 * i + c, (2 * i + c) % AHEAD, (2 * i, 2 * i + 1), h_hi, h_lo, c * KU, DK)
                pe.wait_ge(glrw_split, l + 1)
                pe.wait_ge(glu_done, l * CK + 2)
                for k in range(DK):
                    mm = three(bank[0][0:RANK, :], glr_hi[:, k, :], glr_lo[:, k, :], h_hi[:, k, :], h_lo[:, k, :],
                               k == 0, k == DK - 1)
                mm.then_inc(glr_done, 1)
                for c in range(2):
                    unit(base + 8 + c, c, (2, 3), h_hi, h_lo, c * KU, DK)
                pe.wait_ge(glr_out, l + 1)
                for t in range(2):
                    mm = nc.tensor.matmul(bank[t][:], up_w[:, t * P:(t + 1) * P], glr[:], start=True, stop=True)
                    mm.then_inc(z_done, 1)
                pe.wait_ge(glu_done, l * CK + CK)
                for c in range(2):
                    unit(base + 10 + c, 2 + c, (4, 5), h_hi, h_lo, c * KU, DK)
                pe.wait_ge(soft, l * 8 + 2)
                vbank = (6, 7, 0, 1)
                for half in range(2):
                    for c in range(2):
                        pe.wait_ge(w_split, base + 12 + 2 * half + c + 1 + AHEAD)
                        slot = 2 * half + c
                        for tb in range(TB):
                            for k in range(KU):
                                kk = c * KU + k
                                mm = three(bank[vbank[tb]][:, half * CU:(half + 1) * CU],
                                           h_hi[:, kk, tb * P:(tb + 1) * P], h_lo[:, kk, tb * P:(tb + 1) * P],
                                           w_hi[:, slot, k, :], w_lo[:, slot, k, :], kk == 0, kk == DK - 1)
                        mm.then_inc(w_used, 1)
                pe.wait_ge(qk_done, l * 10 + 10)
                for t in range(2):
                    for b in range(TB):
                        mm = nc.tensor.transpose(bank[4 + t][:, b * P:(b + 1) * P], k_end[:, t, b * P:(b + 1) * P], ident[:])
                    mm.then_inc(kT_mm, 1)
                for c in range(2):
                    unit(base + 16 + c, c, (2, 3), h_hi, h_lo, c * KU, DK)

                def scores(h):
                    t, s = h // 2, h % 2
                    rows = slice(CHUNK * s, CHUNK * s + CHUNK)
                    fwd, bwd = (6, 7) if s == 0 else (0, 1)
                    for kk, qq, into in ((k_fwd, q_fwd, fwd), (k_bwd, q_bwd, bwd)):
                        for b in range(TB):
                            mm = nc.tensor.matmul(bank[into][:, b * P:(b + 1) * P], kk[rows, t, b * P:(b + 1) * P],
                                                  qq[rows, t, b * P:(b + 1) * P], start=True, stop=True)
                    mm.then_inc(att_mm, 1)

                pe.wait_ge(v_out, l * TB + TB)
                scores(0)
                scores(1)
                pe.wait_ge(kT_out, l * 2 + 2)
                unit(base + 18, 2, (4, 5), h_hi, h_lo, 0, DK)
                pe.wait_ge(r_out, l * HEADS + 2)
                pe.wait_ge(tap_done, (l + 1) * 2 * TAPS)
                pe.wait_ge(pool_tap, (l + 1) * 2 * (TAPS - 1))
                for i in range(CK):
                    mm = nc.tensor.matmul(bank[2][:], ones[:], conv[:, i, :], start=i == 0, stop=i == CK - 1)
                mm.then_inc(mean_mm, 1)
                pe.wait_ge(att_sel, l * 8 + 4)
                scores(2)
                scores(3)
                unit(base + 19, 3, (4, 5), h_hi, h_lo, KU, DK)
                for i in range(CK):
                    pe.wait_ge(c_sq, l * CK + i + 1)
                    mm = column_sums(3, 0, glu[:, i, PAD:PAD + T], i == 0, i == CK - 1)
                mm.then_inc(var_mm, 1)

                def within(h):
                    for b in range(TB):
                        nc.tensor.matmul(bank[h][:, b * P:(b + 1) * P], v[:, b, h * P:(h + 1) * P],
                                         att[:, h, b * P:(b + 1) * P], start=b == 0, stop=False, skip_group_check=True)

                pe.wait_ge(att_sel, l * 8 + 8)
                pe.wait_ge(r_out, l * HEADS + HEADS)
                within(0)
                within(1)
                pe.wait_ge(ln_inv, l * 2 + 2)
                nc.tensor.matmul(bank[2][:], ones[:], bc[:, 0, :], start=True, stop=True).then_inc(ln_spread, 1)
                for t in range(2):
                    for odd in range(2):
                        for s in range(2):
                            for b in range(TB - odd):
                                rows = slice(CHUNK * odd, CHUNK * odd + CHUNK)
                                mm = nc.tensor.matmul(
                                    bank[6 - 2 * t + odd][CHUNK * s:CHUNK * s + CHUNK, b * P:(b + 1) * P],
                                    k_endT[rows, t, b * P + CHUNK * s:b * P + CHUNK * s + CHUNK],
                                    v[rows, b, (2 * t + s) * P:(2 * t + s + 1) * P], start=True, stop=True)
                    mm.then_inc(u_mm, 1)
                pe.wait_ge(ln_done, l * CK + CK)
                within(2)
                within(3)
                for h in range(HEADS):
                    t, s = h // 2, h % 2
                    rows = slice(CHUNK * s, CHUNK * s + CHUNK)
                    pe.wait_ge(st, (l * 2 + t + 1) * (NCHUNK - 1))
                    for c in range(1, NCHUNK):
                        mm = nc.tensor.matmul(bank[h][:, c * CHUNK:(c + 1) * CHUNK], state[rows, t, c - 1, :],
                                              q_fwd[rows, t, c * CHUNK:(c + 1) * CHUNK], start=False, stop=c == NCHUNK - 1,
                                              skip_group_check=True)
                    mm.then_inc(o_mm, 1)
                out = base + ZIN_UNITS
                pe.wait_ge(y_ready, l * DK + CK)
                unit(out, 0, (4, 5), h_hi, h_lo, 0, DK)
                pe.wait_ge(o_gated, l * HEADS + 1)
                for h in range(HEADS):
                    pe.wait_ge(o_sq, l * HEADS + h + 1)
                    mm = column_sums(0, h * TB, o_square(h), h == 0, h == HEADS - 1)
                mm.then_inc(oss_mm, 1)
                pe.wait_ge(w_split, out + 1 + 1 + AHEAD)

                def conv_half(k):
                    for m in range(2):
                        mm = three(bank[6 + m][:], w_hi[:, 1, k, m * P:(m + 1) * P], w_lo[:, 1, k, m * P:(m + 1) * P],
                                   h_hi[:, k, :], h_lo[:, k, :], k == 0, False)
                    return mm

                conv_half(0)
                conv_half(1)
                for h in range(HEADS):
                    pe.wait_ge(o_diag, l * HEADS + h + 1)
                    nc.tensor.matmul(bank[h][:], ones[:], att[:, h, :], start=True, stop=True).then_inc(o_spread, 1)
                conv_half(2)
                conv_half(3).then_inc(w_used, 1)
                unit_as_ready(out + 2, 2, (4, 5), h_hi, h_lo, KU, DK, y_round, y_ready, l * DK + CK,
                              ends_pair=True)
                unit_by_tile(out + 3, 3, (6, 7), h_hi, h_lo, KU)
                unit(out + 4, 0, (0, 1), h_hi, h_lo, 0, DK)
                unit_by_tile(out + 5, 1, (0, 1), h_hi, h_lo, KU)
                unit(out + 6, 2, (2, 3), h_hi, h_lo, 0, DK)
                unit_by_tile(out + 7, 3, (2, 3), h_hi, h_lo, KU)

            pe.wait_ge(const_ready, CONSTS)
            for b in range(ADA_PRE):
                if b:
                    pe.wait_ge(mod_ready, b)
                pe.wait_ge(pre_mac, (b + 1) * DK)
                for n in range(DK):
                    mm = nc.tensor.matmul(bank[ADA_BANK_IN][:, n:n + 1], ada_acc[:, n * P:(n + 1) * P], ones[:, 0:1],
                                          start=True, stop=True)
                mm.then_inc(ada_sum, 1)
            with pe.Fori(0, LAYERS) as l:
                ffn(l, 0)
                mixer(l)
                ffn(l, 1)
            stat(3 * LAYERS)

        @block.scalar
        def _(act):
            def split(grp, q, tiles=KU, used=True):
                grp, slot = grp + q // AHEAD, q % AHEAD
                act.wait_ge(w_loaded[slot], grp * 16 + 16)
                if used:
                    act.wait_ge(w_used, grp * AHEAD + slot - AHEAD + 1)
                nc.scalar.activation(w_hi[:, slot, 0:tiles, :], raw[:, slot, 0:tiles, :], ACT.Copy).then_inc(w_round, 1)

            def root(n):
                act.wait_ge(stat_ready, n + 1)
                nc.scalar.activation(inv[:], bank[STAT][:, 0:TB], ACT.Sqrt, bias=eps[:, 0:1], scale=1.0 / D).then_inc(rms_root, 1)

            def norm(n, shift):
                root(n)
                for k in range(DK):
                    act.wait_ge(xn_ready, n * DK + k + 1)
                    nc.scalar.activation(h_hi[:, k, :], tmp[:, k % 3, :], ACT.Identity,
                                         bias=mod[:, shift, k:k + 1]).then_inc(h_round, 1)

            def square(m, slot, updates, sums):
                act.wait_ge(x_ready, updates + m + 1)
                act.wait_ge(ssq_ready, sums + m)
                nc.scalar.activation(tmp[:, slot, :], x[:, bass.ds(m, 1), :].rearrange("p k t -> p (k t)"),
                                     ACT.Square).then_inc(sq_ready, 1)

            def ffn(l, f):
                n = l * 3 + 2 * f
                grp = l * (LAYER_UNITS // AHEAD) + FFN_BASE[f] // AHEAD
                done = (l * 2 + f) * FK
                norm(n, 6 * f)

                def in_block(b, first):
                    split(grp + b, AHEAD)
                    split(grp + b, AHEAD + 1)
                    if first:
                        act.wait_ge(h_ready, n * DK + DK)
                    else:
                        act.wait_ge(g_split, done + 2 * b)
                    for i in range(2):
                        nc.scalar.activation(tmp[:, i, :], bank[IN_GATE[i]][:], ACT.Silu).then_inc(silu_done, 1)
                    split(grp + b, AHEAD + 2)
                    split(grp + b, AHEAD + 3)
                    for i in range(2):
                        act.wait_ge(g_ready, done + 2 * b + i + 1)
                        nc.scalar.activation(g_hi[:, bass.ds(2 * b + i, 1), :].rearrange("p k t -> p (k t)"), tmp[:, i, :],
                                             ACT.Copy).then_inc(g_round, 1)

                in_block(0, True)
                with act.Fori(0, (BLOCKS - 1) // 2) as j:
                    for i in range(2):
                        in_block(2 * j + 1 + i, False)
                act.wait_ge(g_split, done + FK)
                with act.Fori(0, PAIRS // 2) as j:
                    for i in range(2):
                        def step(m):
                            q = i * OUT_UNITS + m + AHEAD
                            tiles = FK % KU if q % OUT_UNITS == OUT_UNITS - 1 else KU
                            split(grp + BLOCKS + j * (2 * OUT_UNITS // AHEAD), q, tiles)

                        for m in range(OUT_UNITS - 1):
                            step(m)
                        for t in range(2):
                            square(4 * j + 2 * i + t, t, DK + l * 3 * DK + 2 * f * DK, (n + 1) * DK)
                        step(OUT_UNITS - 1)

            def mixer(l):
                n = l * 3 + 1
                grp = l * (LAYER_UNITS // AHEAD) + MIX_BASE // AHEAD

                def step(u):
                    split(grp, u + AHEAD)

                def products(tile, first, last):
                    s = tile // 2
                    for j in range(first, last):
                        win, w = glu[:, tile, j:j + T], w_dw[:, tile, j:j + 1]
                        if j == 0:
                            nc.scalar.activation(conv[:, tile, :], win, ACT.Identity, bias=b_dw[:, tile:tile + 1],
                                                 scale=w).then_inc(prod_ready, 1)
                            continue
                        a = s * (TAPS - 1) + j - 1
                        if a >= 3:
                            act.wait_ge(pool_tap, l * 2 * (TAPS - 1) + a - 2)
                        nc.scalar.activation(prod[:, a % 3, :], win, ACT.Copy, scale=w).then_inc(prod_ready, 1)

                norm(n, 3)
                step(0)
                step(1)
                act.wait_ge(mixp_loaded, l * 64 + 64)
                nc.scalar.activation(glr_hi[:], glr_raw[:], ACT.Copy).then_inc(glrw_round, 1)
                step(2)
                step(3)
                act.wait_ge(h_ready, n * DK + DK)
                for i in range(2):
                    nc.scalar.activation(tmp[:, i, :], bank[2 + i][:], ACT.Sigmoid).then_inc(sig_done, 1)
                step(4)
                act.wait_ge(built, l * BUILDS + BUILDS)
                act.wait_ge(glu_done, l * CK + 2)
                products(1, 0, 4)
                for u in range(5, 8):
                    step(u)
                    if u < 7:
                        products(1, 4 * (u - 4), 4 * (u - 3))
                for i in range(2):
                    nc.scalar.activation(tmp[:, i, :], bank[6 + i][:], ACT.Sigmoid).then_inc(sig_done, 1)
                products(1, 12, 16)
                act.wait_ge(glr_done, l + 1)
                nc.scalar.activation(glr[:], bank[0][0:RANK, :], ACT.Copy).then_inc(glr_out, 1)
                products(1, 16, 18)
                step(8)
                products(1, 18, 21)
                step(9)
                act.wait_ge(z_done, l * 2 + 2)
                for t in range(2):
                    nc.scalar.activation(k_fwd[:, t, :], bank[t][:], ACT.Identity, bias=b_gate[:, t:t + 1]).then_inc(soft, 1)
                for t in range(2):
                    act.wait_ge(soft, l * 8 + 1 + t)
                    nc.scalar.activation(k_bwd[:, t, :], k_fwd[:, t, :], ACT.Abs).then_inc(soft, 1)
                for t in range(2):
                    act.wait_ge(soft, l * 8 + 3 + t)
                    nc.scalar.activation(k_bwd[:, t, :], k_bwd[:, t, :], ACT.Exp, scale=-1.0).then_inc(soft, 1)
                for t in range(2):
                    act.wait_ge(soft, l * 8 + 5 + t)
                    nc.scalar.activation(k_bwd[:, t, :], k_bwd[:, t, :], ACT.Ln, bias=1.0).then_inc(soft, 1)
                products(1, 21, 25)
                step(10)
                for t in range(2):
                    act.wait_ge(diff, l * 2 + t + 1)
                    ends = bc[:, t, :].rearrange("p (c j) -> p c j", j=CHUNK)[:, :, CHUNK - 1:CHUNK]
                    nc.scalar.activation(k_bwd[:, t, :], bc[:, t, :], ACT.Exp, scale=1.0 / TAU).then_inc(exps, 1)
                    nc.scalar.activation(k_fwd[:, t, :], bc[:, t, :], ACT.Exp, scale=-1.0 / TAU).then_inc(exps, 1)
                    nc.scalar.activation(k_end[:, t, :], k_end[:, t, :], ACT.Exp, scale=1.0 / TAU).then_inc(exps, 1)
                    nc.scalar.activation(end_exp[:, t, :], ends, ACT.Exp, scale=1.0 / TAU).then_inc(exps, 1)
                products(1, 25, 28)
                step(11)
                products(1, 28, 31)
                for u in range(12, 16):
                    step(u)
                    if u < 15:
                        products(3, 5 * (u - 12), 5 * (u - 11))
                for tb, b in enumerate((6, 7, 0, 1)):
                    nc.scalar.activation(v[:, tb, :], bank[b][:], ACT.Copy).then_inc(v_out, 1)
                for t in range(2):
                    act.wait_ge(kT_mm, l * 2 + t + 1)
                    nc.scalar.activation(k_endT[:, t, :], bank[4 + t][:], ACT.Copy).then_inc(kT_out, 1)
                products(3, 15, 20)
                step(16)
                products(3, 20, 26)
                step(17)
                for i in range(2):
                    nc.scalar.activation(r_act[:, i, :], bank[2 + i][:], ACT.Silu).then_inc(r_out, 1)
                products(3, 26, 31)
                step(18)
                for i in range(CK):
                    act.wait_ge(centred, l * CK + i + 1)
                    nc.scalar.activation(glu[:, i, PAD:PAD + T], conv[:, i, :], ACT.Square).then_inc(c_sq, 1)
                step(19)
                for i in range(2):
                    nc.scalar.activation(r_act[:, 2 + i, :], bank[4 + i][:], ACT.Silu).then_inc(r_out, 1)
                act.wait_ge(var_mm, l + 1)
                nc.scalar.activation(inv[:], bank[3][:, 0:TB], ACT.Sqrt, bias=eps[:, 0:1],
                                     scale=1.0 / (CK * P)).then_inc(ln_root, 1)
                for i in range(CK):
                    act.wait_ge(ln_done, l * CK + i + 1)
                    nc.scalar.activation(conv[:, i, :], conv[:, i, :], ACT.Silu, bias=b_ln[:, i:i + 1],
                                         scale=g_ln[:, i:i + 1]).then_inc(c_act_done, 1)
                for i in range(CK):
                    act.wait_ge(c_act_done, l * CK + i + 1)
                    nc.scalar.activation(h_hi[:, i, :], conv[:, i, :], ACT.Copy).then_inc(y_round, 1)
                for h in range(HEADS):
                    act.wait_ge(o_mm, l * HEADS + h + 1)
                    nc.scalar.activation(o_square(h), bank[h][:], ACT.Square).then_inc(o_sq, 1)
                act.wait_ge(oss_mm, l + 1)
                nc.scalar.activation(inv_o[:].rearrange("p h b -> p (h b)"), bank[0][:, 0:HEADS * TB], ACT.Sqrt,
                                     bias=eps[:, 0:1], scale=1.0 / P).then_inc(o_root, 1)
                step(20)
                for h in range(HEADS):
                    act.wait_ge(o_norm, l * HEADS + h + 1)
                    nc.scalar.activation(h_hi[:, CK + h, :], v[:, h, :], ACT.Copy).then_inc(y_round, 1)
                step(21)
                for p_, steps in enumerate(((22,), (23,), (24, 25), (26, 27))):
                    for u in steps[:-1]:
                        step(u)
                    for t in range(2):
                        square(2 * p_ + t, t, DK + l * 3 * DK + DK, (n + 1) * DK)
                    step(steps[-1])

            act.wait_ge(const_ready, CONSTS)
            act.wait_ge(par_loaded, 48)
            nc.scalar.activation(c_act[:], c_act[:], ACT.Silu).then_inc(c_ready, 1)
            act.wait_ge(x_loaded, 16)
            act.wait_ge(w_split, AHEAD)
            for k in range(DK):
                if k >= 1:
                    act.wait_ge(ssq_ready, k)
                nc.scalar.activation(tmp[:, k % 2, :], x[:, k, :], ACT.Square).then_inc(sq_ready, 1)
            for q in range(AHEAD):
                split(0, q, used=False)
            with act.Fori(0, LAYERS) as l:
                ffn(l, 0)
                mixer(l)
                ffn(l, 1)
            root(3 * LAYERS)
            for k in range(DK):
                act.wait_ge(xn_ready, 3 * LAYERS * DK + k + 1)
                nc.scalar.activation(x[:, k, :], tmp[:, k % 3, :], ACT.Identity,
                                     bias=mod[:, 0, k:k + 1]).then_inc(final_ready, 1)

        @block.vector
        def _(dve):
            def split(grp, q, tiles=KU):
                grp, slot = grp + q // AHEAD, q % AHEAD
                dve.wait_ge(w_round, grp * AHEAD + slot + 1)
                nc.vector.tensor_tensor(w_lo[:, slot, 0:tiles, :], raw[:, slot, 0:tiles, :],
                                        w_hi[:, slot, 0:tiles, :].bitcast(F32), ALU.subtract).then_inc(w_split, 1)

            def add_slice(blk, k):
                dve.wait_ge(ada_loaded[k % ADA_SLOTS], ((blk - ADA_PRE) * (DK // ADA_SLOTS) + k // ADA_SLOTS) * 16 + 16)
                src = ada_raw[:, k % ADA_SLOTS, :]
                if k == 0:
                    dve.wait_ge(ada_sum, blk)
                    nc.vector.tensor_scalar(ada_acc[:], src, c_act[:, k:k + 1], None, ALU.mult).then_inc(ada_mac, 1)
                else:
                    dve.wait_ge(ada_mac, (blk - ADA_PRE) * DK + k + ADA_SLOTS)
                    nc.vector.scalar_tensor_tensor(ada_acc[:], src, c_act[:, k:k + 1], ada_acc[:], ALU.mult,
                                                   ALU.add).then_inc(ada_mac, 1)

            def finish_ada(blk, into, at):
                dve.wait_ge(ada_sum, blk + 1)
                nc.vector.tensor_tensor(mod[:, bass.ds(at, 1), :].rearrange("p a k -> p (a k)"), bank[into][:, 0:DK],
                                        b_ada[:, bass.ds(blk, 1), :].rearrange("p a k -> p (a k)"), ALU.add).then_inc(mod_ready, 1)

            def on_diagonals(out, column):
                return nc.vector.tensor_tensor(out.rearrange("p (b i) -> p b i", i=P),
                                               ident[:].rearrange("p (o i) -> p o i", o=1).to_broadcast([P, TB, P]),
                                               column.rearrange("p (b o) -> p b o", o=1).to_broadcast([P, TB, P]), ALU.mult)

            def inv_rms(n, scale_at, mods):
                dve.wait_ge(mod_ready, mods)
                nc.vector.scalar_tensor_tensor(gain[:], mod[:, scale_at, :], 1.0,
                                               g_norm[:, bass.ds(n, 1), :].rearrange("p a k -> p (a k)"), ALU.add,
                                               ALU.mult).then_inc(gain_ready, 1)
                dve.wait_ge(rms_root, n + 1)
                nc.vector.reciprocal(inv[:], inv[:]).then_inc(rms_step, 1)
                dve.wait_ge(rms_step, 2 * n + 1)
                on_diagonals(ssq[:], inv[:]).then_inc(rms_step, 1)
                dve.wait_ge(gain_ready, n + 1)
                dve.wait_ge(spread, n + 1)

            def scale_x(n, k):
                nc.vector.scalar_tensor_tensor(tmp[:, k % 3, :], x[:, k, :], gain[:, k:k + 1], bank[SPREAD][:], ALU.mult,
                                               ALU.mult).then_inc(xn_ready, 1)

            def norm(n, shift, scale_at, mods):
                inv_rms(n, scale_at, mods)
                for k in range(DK + 1):
                    if k < DK:
                        if k >= 3:
                            dve.wait_ge(h_ready, n * DK + k - 2)
                        scale_x(n, k)
                    if k >= 1:
                        dve.wait_ge(h_round, n * DK + k)
                        nc.vector.scalar_tensor_tensor(h_lo[:, k - 1, :], tmp[:, (k - 1) % 3, :], mod[:, shift, k - 1:k],
                                                       h_hi[:, k - 1, :].bitcast(F32), ALU.add, ALU.subtract).then_inc(h_ready, 1)

            def add_squares(slot, at):
                dve.wait_ge(sq_ready, at)
                dve.wait_ge(ssq_ready, at)
                nc.vector.tensor_tensor(ssq[:], ssq[:], tmp[:, 1 - slot, :], ALU.add).then_inc(ssq_ready, 1)

            def clear_sums():
                nc.vector.memset(ssq[:], 0.0).then_inc(gate_ready, 1)
                nc.vector.memset(tmp[:, 1, :], 0.0).then_inc(gate_ready, 1)

            def update(m, b, gate_col):
                xm = x[:, bass.ds(m, 1), :].rearrange("p k t -> p (k t)")
                nc.vector.scalar_tensor_tensor(xm, bank[b][:], gate_col, xm, ALU.mult, ALU.add).then_inc(x_ready, 1)

            def ffn(l, f):
                n = l * 3 + 2 * f
                grp = l * (LAYER_UNITS // AHEAD) + FFN_BASE[f] // AHEAD
                done = (l * 2 + f) * FK
                norm(n, 6 * f, 6 * f + 1, l * N_MOD + ADA_PRE + f * (ADA_IN + ADA_OUT))

                def in_block(b, blk, k0):
                    for m in range(4):
                        if m < 3:
                            split(grp + b, AHEAD + m)
                        if blk is not None:
                            add_slice(blk, k0 + m)
                    split(grp + b, AHEAD + 3)
                    for i in range(2):
                        dve.wait_ge(silu_done, done + 2 * b + i + 1)
                        nc.vector.tensor_tensor(tmp[:, i, :], tmp[:, i, :], bank[IN_UP[i]][:], ALU.mult).then_inc(g_ready, 1)
                    for i in range(2):
                        m = bass.ds(2 * b + i, 1)
                        dve.wait_ge(g_round, done + 2 * b + i + 1)
                        nc.vector.tensor_tensor(g_lo[:, m, :].rearrange("p k t -> p (k t)"), tmp[:, i, :],
                                                g_hi[:, m, :].rearrange("p k t -> p (k t)").bitcast(F32),
                                                ALU.subtract).then_inc(g_split, 1)

                in_block(0, None, 0)
                with dve.Fori(0, (BLOCKS - 1) // 2) as j:
                    blk = l * N_MOD + j + ADA_PRE
                    for i in range(2):
                        in_block(2 * j + 1 + i, blk if f == 0 else None, 4 * i)
                    if f == 0:
                        finish_ada(blk, ADA_BANK_IN, j + ADA_PRE)
                dve.wait_ge(mod_ready, l * N_MOD + ADA_PRE + ADA_IN + f * ADA_OUT)
                nc.vector.tensor_scalar(gate[:], mod[:, 2 + 6 * f, :], 0.5, None, ALU.mult).then_inc(gate_ready, 1)
                dve.wait_ge(g_split, done + FK)
                clear_sums()
                with dve.Fori(0, PAIRS // 2) as j:
                    blk = l * N_MOD + j + ADA_PRE + ADA_IN + f * ADA_OUT
                    for i in range(2):
                        def step(m):
                            q = i * OUT_UNITS + m + AHEAD
                            tiles = FK % KU if q % OUT_UNITS == OUT_UNITS - 1 else KU
                            split(grp + BLOCKS + j * (2 * OUT_UNITS // AHEAD), q, tiles)

                        for m in range(OUT_UNITS - 1):
                            step(m)
                            if m < 4:
                                add_slice(blk, 4 * i + m)
                        dve.wait_ge(gate_ready, l * 8 + 5 * f + 3)
                        for t in range(2):
                            m = 4 * j + 2 * i + t
                            if t == 0:
                                dve.wait_ge(even_done, l * 3 * PAIRS + 2 * f * PAIRS + 2 * j + i + 1)
                            else:
                                dve.wait_ge(w_used, l * LAYER_UNITS + FFN_BASE[f] + IN_UNITS + (2 * j + i + 1) * OUT_UNITS)
                            update(m, (OUT_A, OUT_B)[i][t], gate[:, bass.ds(m, 1)])
                            add_squares(t, (n + 1) * DK + m)
                        step(OUT_UNITS - 1)
                    finish_ada(blk, ADA_BANK_OUT, j + (ADA_PRE + ADA_IN if f == 0 else 0))

            def mixer(l):
                n = l * 3 + 1
                grp = l * (LAYER_UNITS // AHEAD) + MIX_BASE // AHEAD

                def step(u):
                    split(grp, u + AHEAD)

                def conv_taps(tile, first, last):
                    for j in range(first, last):
                        win, w = glu[:, tile, j:j + T], w_dw[:, tile, j:j + 1]
                        if j == 0:
                            ins = nc.vector.tensor_scalar(conv[:, tile, :], win, w, b_dw[:, tile:tile + 1], ALU.mult, ALU.add)
                        else:
                            dve.wait_ge(tap_done, l * 2 * TAPS + tile // 2 * TAPS + j)
                            ins = nc.vector.scalar_tensor_tensor(conv[:, tile, :], win, w, conv[:, tile, :], ALU.mult, ALU.add)
                        ins.then_inc(tap_done, 1)

                norm(n, 3, 4, l * N_MOD + ADA_PRE + ADA_IN + ADA_OUT)
                step(0)
                step(1)
                dve.wait_ge(glrw_round, l + 1)
                nc.vector.tensor_tensor(glr_lo[:], glr_raw[:], glr_hi[:].bitcast(F32), ALU.subtract).then_inc(glrw_split, 1)
                step(2)
                step(3)
                for i in range(2):
                    dve.wait_ge(sig_done, l * CK + i + 1)
                    nc.vector.tensor_tensor(glu[:, i, PAD:PAD + T], tmp[:, i, :], bank[i][:], ALU.mult).then_inc(glu_done, 1)
                dve.wait_ge(built, l * BUILDS + BUILDS)
                dve.wait_ge(glu_done, l * CK + 2)
                for u in range(4, 7):
                    step(u)
                    conv_taps(0, 5 * (u - 4), 5 * (u - 3))
                step(7)
                for i in range(2):
                    dve.wait_ge(sig_done, l * CK + 2 + i + 1)
                    nc.vector.tensor_tensor(glu[:, 2 + i, PAD:PAD + T], tmp[:, i, :], bank[4 + i][:], ALU.mult).then_inc(glu_done, 1)
                conv_taps(0, 15, 20)
                step(8)
                conv_taps(0, 20, 23)
                step(9)
                for t in range(2):
                    dve.wait_ge(soft, l * 8 + 7 + t)
                    nc.vector.scalar_tensor_tensor(q_fwd[:, t, :], k_fwd[:, t, :], 0.0, k_bwd[:, t, :], ALU.min,
                                                   ALU.subtract).then_inc(logsig, 1)
                for t in range(2):
                    dve.wait_ge(logsig, l * 2 + t + 1)
                    nc.vector.tensor_tensor_scan(bc[:, t, :], restart[:], q_fwd[:, t, :], 0.0, ALU.mult, ALU.add).then_inc(scanned, 1)
                for t in range(2):
                    dve.wait_ge(scanned, l * 2 + t + 1)
                    b3 = bc[:, t, :].rearrange("p (c j) -> p c j", j=CHUNK)
                    nc.vector.tensor_tensor(k_end[:, t, :].rearrange("p (c j) -> p c j", j=CHUNK),
                                            b3[:, :, CHUNK - 1:CHUNK].to_broadcast([P, NCHUNK, CHUNK]), b3,
                                            ALU.subtract).then_inc(diff, 1)
                step(10)
                conv_taps(0, 23, 27)
                dve.wait_ge(exps, l * 8 + 8)
                for t in range(2):
                    for out, ex in ((q_fwd, k_bwd), (q_bwd, k_fwd)):
                        nc.vector.scalar_tensor_tensor(out[:, t, :], bank[2 + t][:], CHUNK ** -0.5, ex[:, t, :], ALU.mult,
                                                       ALU.mult).then_inc(qk_done, 1)
                step(11)
                for t in range(2):
                    for ex in (k_bwd, k_fwd, k_end):
                        nc.vector.tensor_tensor(ex[:, t, :], ex[:, t, :], bank[4 + t][:], ALU.mult).then_inc(qk_done, 1)
                conv_taps(0, 27, 31)
                for u in range(12, 18):
                    step(u)
                    conv_taps(2, 5 * (u - 12), min(5 * (u - 11), TAPS - 2))

                def select(mask, heads, banks):
                    for h, b in zip(heads, banks):
                        where = mask[:].bitcast(U32).rearrange("p (o i) -> p o i", o=1).to_broadcast([P, TB, P])
                        nc.vector.copy_predicated(att[:, h, :].rearrange("p (b i) -> p b i", i=P), where,
                                                  bank[b][:].rearrange("p (b i) -> p b i", i=P)).then_inc(att_sel, 1)

                def centre(i):
                    nc.vector.scalar_tensor_tensor(conv[:, i, :], bank[2][:], -1.0 / (CK * P), conv[:, i, :], ALU.mult,
                                                   ALU.add).then_inc(centred, 1)

                dve.wait_ge(att_mm, l * HEADS + 2)
                conv_taps(2, TAPS - 2, TAPS - 1)
                select(mask_f, (0, 1), (6, 0))
                dve.wait_ge(att_sel, l * 8 + 2)
                conv_taps(2, TAPS - 1, TAPS)
                select(mask_b, (0, 1), (7, 1))
                step(18)
                dve.wait_ge(mean_mm, l + 1)
                centre(0)
                centre(1)
                dve.wait_ge(att_mm, l * HEADS + HEADS)
                centre(2)
                select(mask_f, (2, 3), (6, 0))
                dve.wait_ge(att_sel, l * 8 + 6)
                centre(3)
                select(mask_b, (2, 3), (7, 1))
                step(19)
                dve.wait_ge(ln_root, l + 1)
                nc.vector.reciprocal(inv[:], inv[:]).then_inc(ln_inv, 1)
                dve.wait_ge(ln_inv, l * 2 + 1)
                on_diagonals(bc[:, 0, :], inv[:]).then_inc(ln_inv, 1)
                dve.wait_ge(ln_spread, l + 1)
                for i in range(CK):
                    nc.vector.tensor_tensor(conv[:, i, :], conv[:, i, :], bank[2][:], ALU.mult).then_inc(ln_done, 1)
                for t in range(2):
                    dve.wait_ge(u_mm, l * 2 + t + 1)
                    for c in range(NCHUNK - 1):
                        u = bank[6 - 2 * t + c % 2][:, (c // 2) * P:(c // 2 + 1) * P]
                        if c == 0:
                            ins = nc.vector.tensor_copy(state[:, t, 0, :], u)
                        else:
                            dve.wait_ge(st, (l * 2 + t) * (NCHUNK - 1) + c)
                            ins = nc.vector.scalar_tensor_tensor(state[:, t, c, :], state[:, t, c - 1, :], end_exp[:, t, c:c + 1],
                                                                 u, ALU.mult, ALU.add)
                        ins.then_inc(st, 1)
                for i in range(CK):
                    dve.wait_ge(y_round, l * DK + i + 1)
                    nc.vector.tensor_tensor(h_lo[:, i, :], conv[:, i, :], h_hi[:, i, :].bitcast(F32), ALU.subtract).then_inc(y_ready, 1)
                clear_sums()
                for h in range(HEADS):
                    dve.wait_ge(o_sq, l * HEADS + h + 1)
                    nc.vector.scalar_tensor_tensor(v[:, h, :], bank[h][:], g_gla[:, h:h + 1], r_act[:, h, :], ALU.mult,
                                                   ALU.mult).then_inc(o_gated, 1)
                dve.wait_ge(o_root, l + 1)
                nc.vector.reciprocal(inv_o[:], inv_o[:]).then_inc(o_inv, 1)
                dve.wait_ge(o_inv, l + 1)
                for h in range(HEADS):
                    on_diagonals(att[:, h, :], inv_o[:, h, :]).then_inc(o_diag, 1)
                step(20)
                for h in range(HEADS + 1):
                    if h < HEADS:
                        dve.wait_ge(o_spread, l * HEADS + h + 1)
                        nc.vector.tensor_tensor(v[:, h, :], v[:, h, :], bank[h][:], ALU.mult).then_inc(o_norm, 1)
                    if h:
                        dve.wait_ge(y_round, l * DK + CK + h)
                        nc.vector.tensor_tensor(h_lo[:, CK + h - 1, :], v[:, h - 1, :], h_hi[:, CK + h - 1, :].bitcast(F32),
                                                ALU.subtract).then_inc(y_ready, 1)
                step(21)
                dve.wait_ge(gate_ready, l * 8 + 5)
                for p_, steps in enumerate(((22,), (23,), (24, 25), (26, 27))):
                    for u in steps[:-1]:
                        step(u)
                    for t in range(2):
                        m = 2 * p_ + t
                        if t == 0:
                            dve.wait_ge(even_done, l * 3 * PAIRS + PAIRS + p_ + 1)
                        else:
                            dve.wait_ge(w_used, l * LAYER_UNITS + MIX_BASE + steps[-1] + 1)
                        update(m, (4, 6, 0, 2)[p_] + t, mod[:, 5, m:m + 1])
                        add_squares(t, (n + 1) * DK + m)
                    step(steps[-1])

            nc.vector.memset(ssq[:], 0.0).then_inc(ada_mac, ADA_SLOTS)
            nc.vector.memset(gain[:, 0:1], 0.0).then_inc(x_ready, DK)
            nc.vector.memset(tmp[:, 1, :], 0.0).then_inc(w_split, AHEAD)
            dve.wait_ge(ada_mac, ADA_SLOTS)
            dve.wait_ge(w_split, AHEAD)
            for k in range(DK):
                if k:
                    dve.wait_ge(sq_ready, k)
                    dve.wait_ge(ssq_ready, k)
                nc.vector.tensor_tensor(ssq[:], ssq[:], tmp[:, 1 - k % 2, :], ALU.add).then_inc(ssq_ready, 1)
            dve.wait_ge(c_ready, 1)
            for b in range(ADA_PRE):
                for k in range(DK):
                    dve.wait_ge(pre_loaded[b * DK + k], 16)
                    if k == 0:
                        if b:
                            dve.wait_ge(ada_sum, b)
                        nc.vector.tensor_scalar(ada_acc[:], pre[:, b, k, :], c_act[:, k:k + 1], None, ALU.mult).then_inc(pre_mac, 1)
                    else:
                        dve.wait_ge(pre_mac, b * DK + k)
                        nc.vector.scalar_tensor_tensor(ada_acc[:], pre[:, b, k, :], c_act[:, k:k + 1], ada_acc[:], ALU.mult,
                                                       ALU.add).then_inc(pre_mac, 1)
                finish_ada(b, ADA_BANK_IN, b)
            for q in range(AHEAD):
                split(0, q)
            with dve.Fori(0, LAYERS) as l:
                ffn(l, 0)
                mixer(l)
                ffn(l, 1)
            inv_rms(3 * LAYERS, 1, LAYERS * N_MOD + ADA_PRE)
            for k in range(DK):
                if k >= 3:
                    dve.wait_ge(final_ready, k - 2)
                scale_x(3 * LAYERS, k)


def kernel(**inputs):
    import numpy as np
    import concourse.bacc as bacc
    from concourse import mybir as mb
    from concourse.bass_utils import run_bass_kernel_spmd

    a = {n: np.asarray(v) for n, v in inputs.items()}
    L = LAYERS

    def columns(z):
        z = z.reshape(*z.shape[:-1], -1, P)
        return np.moveaxis(z, -1, 0)

    laid = {
        "xT": a["x"][0].T,
        "cT": columns(a["c"][0]),
        "w_ada": np.concatenate([*a["w_ada"], a["w_ada_final"]], axis=1),
        "b_adaT": columns(np.concatenate([a["b_ada"].reshape(-1), a["b_ada_final"]]).reshape(-1, D)),
        "g_normT": columns(np.stack([z for l in range(L) for z in (a["g_norm_ffn1"][l], a["g_norm_mix"][l], a["g_norm_ffn2"][l])]
                                    + [a["g_norm_final"]])),
        "w_ffn1_in": a["w_ffn1_in"], "w_ffn1_out": a["w_ffn1_out"], "w_in": a["w_in"],
        "w_glr": np.moveaxis(a["w_in"][:, :, GLR_COL:].reshape(L * DK, P, RANK), 1, 0),
        "w_ffn2_in": a["w_ffn2_in"], "w_ffn2_out": a["w_ffn2_out"], "w_out": a["w_out"],
        "w_dwT": np.moveaxis(columns(a["w_dw"]), 2, 3),
        "mix_colsT": np.concatenate([columns(a[n]) for n in ("b_dw", "g_conv_ln", "b_conv_ln", "b_gate")]
                                    + [columns(a["g_gla_norm"].reshape(L, -1))], axis=2),
        "w_gate_up": np.moveaxis(a["w_gate_up"], 1, 0),
    }
    nc = bacc.Bacc("TRN2", target_bir_lowering=False, num_devices=1)
    arrays, args = {}, []
    for name, z in laid.items():
        z = np.ascontiguousarray(z)
        arrays[f"in_{name}"] = z
        args.append(nc.dram_tensor(f"in_{name}", z.shape, mb.dt.from_np(z.dtype), kind="ExternalInput").ap())
    args.append(nc.dram_tensor("out_T", (D, T), F32, kind="ExternalOutput").ap())
    trunk(nc, *args)
    r = run_bass_kernel_spmd(nc, [arrays], core_ids=[0])
    return np.ascontiguousarray(r.results[0]["out_T"].T)[None]
```

```python
from contextlib import ExitStack

import concourse.bass as bass
from concourse import mybir

F32 = mybir.dt.float32
F32R = mybir.dt.float32r
U32 = mybir.dt.uint32
ALU = mybir.AluOpType
ACT = mybir.ActivationFunctionType

P = 128
LAYERS = 2
D = 1024
T = 512
DK = D // P
D_FF = 2816
FK = D_FF // P
N_MOD = 9
SQ = 32
EPS = 1e-6
HEADS = 4
CHUNK = 64
NCHUNK = T // CHUNK
TB = T // P
TAPS = 31
HEAD_TAPS = 10
CK = 4
RANK = 16
TAU = 16.0
D_IN = 2576

KU, CU = 4, 256
AHEAD = 4
BLOCKS = D_FF // CU
PAIRS = D // CU
OUT_UNITS = -(-FK // KU)
IN_UNITS = 4 * BLOCKS
FFN_UNITS = IN_UNITS + PAIRS * OUT_UNITS
ZIN_UNITS = 20
MIX_UNITS = ZIN_UNITS + 2 * PAIRS
LAYER_UNITS = 2 * FFN_UNITS + MIX_UNITS
FFN_BASE = (0, FFN_UNITS + MIX_UNITS)
MIX_BASE = FFN_UNITS
ZIN_COLS = (0, 512, 256, 768, 1024, 1280, 1536, 1792, 2048, 2304)
GLR_COL = 2560
assert IN_UNITS % AHEAD == 0 and (PAIRS * OUT_UNITS) % AHEAD == 0 and MIX_UNITS % AHEAD == 0
assert BLOCKS % 2 == 1 and OUT_UNITS * 2 % AHEAD == 0

MIX_OUT = ((0, 0), (1, 0), (0, 1), (1, 1), (2, 0), (2, 1), (3, 0), (3, 1))

ADA_PRE = 2
ADA_SLOTS = 2
ADA_IN = (BLOCKS - 1) // 2
ADA_OUT = PAIRS // 2
assert ADA_IN + 2 * ADA_OUT == N_MOD


def trunk(nc, xT, cT, w_ada, b_adaT, g_normT, w_ffn1_in, w_ffn1_out, w_in, w_glr, w_ffn2_in, w_ffn2_out, w_out,
          w_dwT, mix_colsT, w_gate_up, outT):
    ffn_in = [w.rearrange("l (c k p) n -> p (l c) k n", p=P, k=KU) for w in (w_ffn1_in, w_ffn2_in)]
    ffn_out = [w.rearrange("l (k p) n -> p (l k) n", p=P) for w in (w_ffn1_out, w_ffn2_out)]
    z_in = w_in.rearrange("l (c k p) n -> p (l c) k n", p=P, k=KU)
    y_out = w_out.rearrange("l (c k p) n -> p (l c) k n", p=P, k=KU)
    ada = w_ada.rearrange("(k p) n -> p k n", p=P)

    with ExitStack() as ctx:
        def sem(name):
            return ctx.enter_context(nc.semaphore(name))

        top = [-(-nc.sbuf_base // 64) * 64]

        def place(name, shape, dt=F32, at=None):
            size = 1
            for n in shape[1:]:
                size *= n
            size *= 4
            off = top[0] if at is None else at[0]
            (top if at is None else at)[0] = off + -(-size // 32) * 32
            return nc.alloc_sbuf_tensor_at(name, shape, dt, offset=off)

        x = place("x", [P, DK, T])
        h_hi = place("h_hi", [P, DK, T], F32R)
        h_lo = place("h_lo", [P, DK, T], F32R)
        raw = place("raw", [P, AHEAD, KU, CU])
        w_hi = place("w_hi", [P, AHEAD, KU, CU], F32R)
        w_lo = place("w_lo", [P, AHEAD, KU, CU], F32R)
        ada_raw = place("ada_raw", [P, ADA_SLOTS, D])
        ada_acc = place("ada_acc", [P, D])
        tmp = place("tmp", [P, 3, T])
        ssq = place("ssq", [P, T])
        inv = place("inv", [P, TB])
        ones = place("ones", [P, P])
        eps = place("eps", [P, 1])
        ident = place("ident", [P, P])
        fold = place("fold", [P, SQ])
        ada_part = place("ada_part", [P, D // SQ])
        mask_f = place("mask_f", [P, P])
        mask_b = place("mask_b", [P, P])
        mod = place("mod", [P, N_MOD, DK])
        b_ada = place("b_ada", [P, LAYERS * N_MOD + 2, DK])
        g_norm = place("g_norm", [P, 3 * LAYERS + 1, DK])
        gain = place("gain", [P, DK])
        gate = place("gate", [P, DK])
        c_act = place("c_act", [P, DK])
        shared = top[0]
        ffn_map = [shared]
        g_hi = place("g_hi", [P, FK, T], F32R, ffn_map)
        g_lo = place("g_lo", [P, FK, T], F32R, ffn_map)
        pre_map = [shared]
        pre = place("pre", [P, ADA_PRE, DK, D], F32, pre_map)
        pre_acc = place("pre_acc", [P, D], F32, pre_map)
        mix_map = [shared]
        PAD = TAPS - 1
        glu = place("glu", [P, CK, PAD + T], F32, mix_map)
        conv = place("conv", [P, CK, T], F32, mix_map)
        bc = place("bc", [P, 2, T], F32, mix_map)
        k_bwd = place("k_bwd", [P, 2, T], F32, mix_map)
        k_fwd = place("k_fwd", [P, 2, T], F32, mix_map)
        k_end = place("k_end", [P, 2, T], F32, mix_map)
        q_fwd = place("q_fwd", [P, 2, T], F32, mix_map)
        q_bwd = place("q_bwd", [P, 2, T], F32, mix_map)
        v = place("v", [P, TB, HEADS * P], F32, mix_map)
        att = place("att", [P, HEADS, T], F32, mix_map)
        k_endT = place("k_endT", [P, 2, T], F32, mix_map)
        prod = place("prod", [P, 3, T], F32, [mix_map[0]])
        state = place("state", [P, 2, NCHUNK - 1, P], F32, mix_map)
        r_act = place("r_act", [P, HEADS, T], F32, mix_map)
        inv_o = place("inv_o", [P, HEADS, TB], F32, mix_map)
        end_exp = place("end_exp", [P, 2, NCHUNK], F32, mix_map)
        w_dw = place("w_dw", [P, CK, TAPS], F32, mix_map)
        cols = place("cols", [P, 18], F32, mix_map)
        glr_raw = place("glr_raw", [P, DK, RANK], F32, mix_map)
        glr_w = place("glr_w", [P, DK, 2 * RANK], F32R, mix_map)
        glr = place("glr", [2 * RANK, T], F32, mix_map)
        up_w = place("up_w", [2 * RANK, 2 * P], F32, mix_map)
        restart = place("restart", [P, T], F32, mix_map)
        assert max(ffn_map[0], pre_map[0], mix_map[0]) <= nc.sbuf_usable_end, (ffn_map, pre_map, mix_map)
        b_dw, g_ln, b_ln, b_gate, g_gla = (cols[:, a:b] for a, b in ((0, 4), (4, 8), (8, 12), (12, 14), (14, 18)))

        bank = [ctx.enter_context(nc.psum_tensor(f"bank{i}", [P, T], F32)) for i in range(8)]
        IN_GATE, IN_UP, OUT_A, OUT_B = (0, 1), (2, 3), (4, 5), (6, 7)
        ADA_BANK_IN, ADA_BANK_OUT, STAT, SPREAD, SPARE = 6, 2, 1, 7, 0
        ADA_BANK_PRE = (6, 2)
        WARM_PRE, WARM_MIX, WARM_NORM = 8, 2, (10, 3, 5)

        w_loaded = [sem(f"w_loaded{s}") for s in range(AHEAD)]
        w_round = sem("w_round")
        w_split = sem("w_split")
        w_used = sem("w_used")
        even_done = sem("even_done")
        par_loaded = sem("par_loaded")
        pre_loaded = [sem(f"pre_loaded{b}") for b in range(ADA_PRE * DK)]
        x_loaded = sem("x_loaded")
        mixp_loaded = sem("mixp_loaded")
        ada_loaded = [sem(f"ada_loaded{s}") for s in range(ADA_SLOTS)]
        ada_mac = sem("ada_mac")
        ada_fold = sem("ada_fold")
        FOLDS = 4
        fold_ready = sem("fold_ready")
        ada_sum = sem("ada_sum")
        mod_ready = sem("mod_ready")
        pre_mac = sem("pre_mac")
        c_ready = sem("c_ready")
        const_ready = sem("const_ready")
        x_ready = sem("x_ready")
        sq_ready = sem("sq_ready")
        ssq_ready = sem("ssq_ready")
        stat_ready = sem("stat_ready")
        rms_root = sem("rms_root")
        rms_step = sem("rms_step")
        spread = sem("spread")
        gain_ready = sem("gain_ready")
        xn_ready = sem("xn_ready")
        h_round = sem("h_round")
        h_ready = sem("h_ready")
        silu_done = sem("silu_done")
        g_ready = sem("g_ready")
        g_round = sem("g_round")
        g_split = sem("g_split")
        gate_ready = sem("gate_ready")
        final_ready = sem("final_ready")
        stored = sem("stored")
        built = sem("built")
        sig_done = sem("sig_done")
        glu_done = sem("glu_done")
        tap_done = {i: sem(f"tap_done{i}") for i in (0, 2, 3)}
        tap_total = {0: TAPS, 2: TAPS, 3: HEAD_TAPS}
        pair_sum = sem("pair_sum")
        sq_sum = sem("sq_sum")
        prod_ready = sem("prod_ready")
        PROD = (TAPS, TAPS - HEAD_TAPS)
        pool_tap = sem("pool_tap")
        glrw_round = sem("glrw_round")
        glrw_split = sem("glrw_split")
        glr_done = sem("glr_done")
        glr_out = sem("glr_out")
        z_done = sem("z_done")
        soft = sem("soft")
        logsig = sem("logsig")
        scanned = sem("scanned")
        diff = sem("diff")
        exps = sem("exps")
        qk_done = sem("qk_done")
        v_out = sem("v_out")
        r_out = sem("r_out")
        att_mm = sem("att_mm")
        att_sel = sem("att_sel")
        kT_mm = sem("kT_mm")
        kT_out = sem("kT_out")
        u_mm = sem("u_mm")
        st = sem("st")
        o_mm = sem("o_mm")
        o_sq = sem("o_sq")
        o_gated = sem("o_gated")
        oss_mm = sem("oss_mm")
        o_root = sem("o_root")
        o_inv = sem("o_inv")
        o_spread = sem("o_spread")
        o_norm = sem("o_norm")
        y_round = sem("y_round")
        y_ready = sem("y_ready")
        mean_mm = sem("mean_mm")
        centred = sem("centred")
        c_sq = sem("c_sq")
        var_mm = sem("var_mm")
        ln_root = sem("ln_root")
        ln_inv = sem("ln_inv")
        ln_spread = sem("ln_spread")
        ln_done = sem("ln_done")
        c_act_done = sem("c_act_done")

        POOL_TAPS = sum(PROD) - 1
        BUILDS = 4
        CONSTS = 11

        def o_square(h):
            return (q_bwd if h < 2 else k_fwd)[:, h % 2, :]

        def o_tile(h):
            return (k_bwd if h < 2 else k_end)[:, h % 2, :]

        block = ctx.enter_context(nc.Block())

        @block.sync
        def _(sp):
            sp.dma_start(c_act[:], cT).then_inc(par_loaded, 16)
            sp.dma_start(b_ada[:], b_adaT).then_inc(par_loaded, 16)
            sp.dma_start(g_norm[:], g_normT).then_inc(par_loaded, 16)
            sp.dma_start(x[:], xT.rearrange("(k p) t -> p k t", p=P)).then_inc(x_loaded, 16)
            for b in range(ADA_PRE):
                for k in range(DK):
                    sp.dma_start(pre[:, b, k, :], ada[:, k, b * D:(b + 1) * D]).then_inc(pre_loaded[b * DK + k], 16)

            def load(unit, slot, src, tiles=KU):
                sp.wait_ge(w_split, unit + 1)
                sp.dma_start(raw[:, slot, 0:tiles, :], src).then_inc(w_loaded[slot], 16)

            def load_block(l, f, base, b, s):
                for half in range(2):
                    for c in range(2):
                        load(base + 4 * b + 2 * half + c, (s + 2 * half + c) % AHEAD,
                             ffn_in[f][:, 2 * l + c, :, bass.ds(b * CU + half * D_FF, CU)])

            def load_ffn(l, f):
                base = l * LAYER_UNITS + FFN_BASE[f]
                load_block(l, f, base, 0, 0)
                with sp.Fori(0, (BLOCKS - 1) // 2) as j:
                    for i in range(2):
                        load_block(l, f, base, 2 * j + 1 + i, 0)
                with sp.Fori(0, PAIRS // 2) as j:
                    for i in range(2):
                        for n in range(OUT_UNITS):
                            tiles = min(KU, FK - n * KU)
                            q = i * OUT_UNITS + n
                            load(base + IN_UNITS + j * 2 * OUT_UNITS + q, q % AHEAD,
                                 ffn_out[f][:, bass.ds(l * FK + n * KU, tiles), bass.ds((2 * j + i) * CU, CU)], tiles)

            with sp.Fori(0, LAYERS) as l:
                load_ffn(l, 0)
                base = l * LAYER_UNITS + MIX_BASE
                for n, col in enumerate(ZIN_COLS):
                    for c in range(2):
                        load(base + 2 * n + c, (2 * n + c) % AHEAD, z_in[:, 2 * l + c, :, col:col + CU])
                for n, (p_, c) in enumerate(MIX_OUT):
                    load(base + ZIN_UNITS + n, n % AHEAD, y_out[:, 2 * l + c, :, p_ * CU:(p_ + 1) * CU])
                load_ffn(l, 1)
            load_block(0, 0, LAYERS * LAYER_UNITS, 0, 0)
            for k in range(DK):
                sp.wait_ge(final_ready, k + 1)
                sp.dma_start(outT[k * P:(k + 1) * P, :], x[:, k, :]).then_inc(stored, 16)
            sp.wait_ge(stored, 16 * DK)

        @block.gpsimd
        def _(pool):
            def load_ada(blk):
                for k in range(DK):
                    pool.wait_ge(ada_mac, (blk - ADA_PRE) * DK + k + 1)
                    pool.dma_start(ada_raw[:, k % ADA_SLOTS, :],
                                   ada[:, k, bass.ds(blk * D, D)]).then_inc(ada_loaded[k % ADA_SLOTS], 16)

            pool.memset(eps[:], EPS).then_inc(const_ready, 1)
            pool.memset(ones[:], 1.0).then_inc(const_ready, 1)
            pool.memset(mask_f[:], 1.0).then_inc(const_ready, 1)
            pool.memset(mask_b[:], 1.0).then_inc(const_ready, 1)
            pool.memset(ident[:], 0.0).then_inc(const_ready, 1)
            pool.wait_ge(const_ready, 5)
            pool.affine_select(out=ident[:], in_=ident[:], compare_op=ALU.not_equal, fill=1.0, base=0,
                               pattern=[[-1, P]], channel_multiplier=1).then_inc(const_ready, 1)
            pool.affine_select(out=mask_f[:], in_=mask_f[:], compare_op=ALU.is_ge, fill=0.0, base=0,
                               pattern=[[1, P]], channel_multiplier=-1).then_inc(const_ready, 1)
            pool.affine_select(out=mask_b[:], in_=mask_b[:], compare_op=ALU.is_ge, fill=0.0, base=-1,
                               pattern=[[-1, P]], channel_multiplier=1).then_inc(const_ready, 1)
            pool.wait_ge(const_ready, 8)
            pool.memset(mask_f[0:CHUNK, CHUNK:P], 0.0).then_inc(const_ready, 1)
            pool.memset(mask_b[CHUNK:P, 0:CHUNK], 0.0).then_inc(const_ready, 1)
            pool.memset(mask_b[0:CHUNK, CHUNK:P], 0.0).then_inc(const_ready, 1)
            pool.wait_ge(pre_mac, ADA_PRE * DK - 4)
            with pool.Fori(0, LAYERS) as l:
                with pool.Fori(0, ADA_IN) as j:
                    load_ada(l * N_MOD + j + ADA_PRE)
                with pool.Fori(0, ADA_OUT) as j:
                    load_ada(l * N_MOD + j + (ADA_PRE + ADA_IN))
                pool.wait_ge(w_used, l * LAYER_UNITS + MIX_BASE)
                pool.dma_start(w_dw[:], w_dwT[:, bass.ds(l, 1), :, :].rearrange("p l c t -> p (l c) t")).then_inc(mixp_loaded, 16)
                pool.dma_start(cols[:], mix_colsT[:, bass.ds(l, 1), :].rearrange("p l c -> p (l c)")).then_inc(mixp_loaded, 16)
                pool.dma_start(glr_raw[:], w_glr[:, bass.ds(l * DK, DK), :]).then_inc(mixp_loaded, 16)
                for i in range(2):
                    pool.dma_start(up_w[i * RANK:(i + 1) * RANK, :],
                                   w_gate_up[:, bass.ds(l, 1), :].rearrange("r l c -> r (l c)")).then_inc(mixp_loaded, 16)
                pool.memset(glu[:, :, 0:PAD], 0.0).then_inc(built, 1)
                pool.memset(att[:], 0.0).then_inc(built, 1)
                by_chunk = restart[:].rearrange("p (c j) -> p c j", j=CHUNK)
                pool.memset(by_chunk[:, :, 0:1], 0.0).then_inc(built, 1)
                pool.memset(by_chunk[:, :, 1:CHUNK], 1.0).then_inc(built, 1)
                for a in range(POOL_TAPS):
                    pool.wait_ge(prod_ready, l * sum(PROD) + a + 2)
                    if a == TAPS - 1:
                        pool.wait_ge(tap_done[3], l * HEAD_TAPS + HEAD_TAPS)
                    if a:
                        pool.wait_ge(pool_tap, l * POOL_TAPS + a)
                    i = 1 if a < TAPS - 1 else 3
                    pool.tensor_tensor(conv[:, i, :], conv[:, i, :], prod[:, a % 3, :], ALU.add).then_inc(pool_tap, 1)
                with pool.Fori(0, ADA_OUT) as j:
                    load_ada(l * N_MOD + j + (ADA_PRE + ADA_IN + ADA_OUT))

        @block.tensor
        def _(pe):
            def three(out, a_hi, a_lo, b_hi, b_lo, first, last):
                nc.tensor.matmul(out, a_hi, b_hi, start=first, stop=False)
                nc.tensor.matmul(out, a_hi, b_lo, start=False, stop=False)
                return nc.tensor.matmul(out, a_lo, b_hi, start=False, stop=last)

            def unit(u, slot, banks, rhs_hi, rhs_lo, k0, total):
                pe.wait_ge(w_split, u + 1 + AHEAD)
                for k in range(KU):
                    for m in range(2):
                        mm = three(bank[banks[m]][:], w_hi[:, slot, k, m * P:(m + 1) * P], w_lo[:, slot, k, m * P:(m + 1) * P],
                                   rhs_hi[:, k0 + k, :], rhs_lo[:, k0 + k, :], k0 + k == 0, k0 + k == total - 1)
                mm.then_inc(w_used, 1)

            def unit_as_ready(u, slot, banks, rhs_hi, rhs_lo, k0, total, rounded, split, at, tiles=KU,
                              ends_pair=False):
                pe.wait_ge(w_split, u + 1 + AHEAD)
                for k in range(tiles):
                    first, last = k0 + k == 0, k0 + k == total - 1
                    w = [(w_hi[:, slot, k, m * P:(m + 1) * P], w_lo[:, slot, k, m * P:(m + 1) * P]) for m in range(2)]
                    pe.wait_ge(rounded, at + k + 1)
                    for m in range(2):
                        nc.tensor.matmul(bank[banks[m]][:], w[m][0], rhs_hi[:, k0 + k, :], start=first, stop=False)
                        nc.tensor.matmul(bank[banks[m]][:], w[m][1], rhs_hi[:, k0 + k, :], start=False, stop=False)
                    pe.wait_ge(split, at + k + 1)
                    for m in range(2):
                        mm = nc.tensor.matmul(bank[banks[m]][:], w[m][0], rhs_lo[:, k0 + k, :], start=False, stop=last)
                        if ends_pair and k == tiles - 1 and m == 0:
                            mm.then_inc(even_done, 1)
                mm.then_inc(w_used, 1)

            def unit_by_tile(u, slot, banks, rhs_hi, rhs_lo, k0, tiles=KU):
                pe.wait_ge(w_split, u + 1 + AHEAD)
                for m in range(2):
                    for k in range(tiles):
                        mm = three(bank[banks[m]][:], w_hi[:, slot, k, m * P:(m + 1) * P], w_lo[:, slot, k, m * P:(m + 1) * P],
                                   rhs_hi[:, k0 + k, :], rhs_lo[:, k0 + k, :], False, k == tiles - 1)
                    if m == 0:
                        mm.then_inc(even_done, 1)
                mm.then_inc(w_used, 1)

            def ada_flush(blk, into):
                pe.wait_ge(ada_fold, (blk - ADA_PRE + 1) * FOLDS)
                pe.wait_ge(mod_ready, blk)
                for r in range(P // SQ):
                    mm = nc.tensor.matmul(bank[into][r * SQ:(r + 1) * SQ, 0:DK], fold[:], ada_part[:, r::P // SQ],
                                          start=True, stop=True)
                mm.then_inc(ada_sum, 1)

            def column_sums(into, col, src, first, last):
                for b in range(TB):
                    mm = nc.tensor.matmul(bank[into][:, col + b:col + b + 1], src[:, b * P:(b + 1) * P], ones[:, 0:1],
                                          start=first and b == 0, stop=last, skip_group_check=True)
                return mm

            def along_tokens(into, column):
                for b in range(TB):
                    mm = nc.tensor.matmul(bank[into][:, b * P:(b + 1) * P], column[:, b:b + 1].to_broadcast([P, P]),
                                          ident[:], start=True, stop=True)
                return mm

            def keep_warm(count, into=SPARE):
                for _ in range(count):
                    nc.tensor.matmul(bank[into][:], ones[:].bitcast(F32R), ones[:, 0:1].bitcast(F32R).to_broadcast([P, T]),
                                     start=True, stop=True)

            def mean_squares(n):
                pe.wait_ge(ssq_ready, (n + 1) * DK)
                column_sums(STAT, 0, ssq, True, False)
                pe.wait_ge(sq_ready, (n + 1) * DK)
                column_sums(STAT, 0, tmp[:, 1, :], False, True).then_inc(stat_ready, 1)

            def spread_rms(n):
                pe.wait_ge(rms_step, n + 1)
                along_tokens(SPREAD, inv).then_inc(spread, 1)

            def stat(n):
                pe.wait_ge(x_ready, n * DK + DK - 2)
                keep_warm(WARM_NORM[0])
                mean_squares(n)
                keep_warm(WARM_NORM[1])
                spread_rms(n)
                keep_warm(WARM_NORM[2])

            def ffn(l, f):
                n = l * 3 + 2 * f
                base = l * LAYER_UNITS + FFN_BASE[f]
                done = (l * 2 + f) * FK

                def in_block(b, first, blk=None):
                    if not first:
                        pe.wait_ge(silu_done, done + 2 * b)
                    for c in range(2):
                        if first:
                            unit_as_ready(base + c, c, IN_GATE, h_hi, h_lo, c * KU, DK, h_round, h_ready, n * DK + c * KU)
                        else:
                            unit(base + 4 * b + c, c, IN_GATE, h_hi, h_lo, c * KU, DK)
                    if not first:
                        pe.wait_ge(g_ready, done + 2 * b)
                    for c in range(2):
                        if c == 1 and blk is not None:
                            ada_flush(blk, ADA_BANK_IN)
                        unit(base + 4 * b + 2 + c, 2 + c, IN_UP, h_hi, h_lo, c * KU, DK)

                in_block(0, True)
                with pe.Fori(0, (BLOCKS - 1) // 2) as j:
                    for i in range(2):
                        in_block(2 * j + 1 + i, False, l * N_MOD + j + ADA_PRE if f == 0 and i == 1 else None)
                with pe.Fori(0, PAIRS // 2) as j:
                    for i in range(2):
                        banks = (OUT_A, OUT_B)[i]
                        pe.wait_ge(x_ready, l * 3 * DK + 2 * f * DK + 4 * j + 2 * i + DK - 2)
                        if i == 1:
                            pe.wait_ge(mod_ready, l * N_MOD + ADA_PRE + ADA_IN + f * ADA_OUT)
                        for m in range(OUT_UNITS):
                            q = i * OUT_UNITS + m
                            u, slot = base + IN_UNITS + j * 2 * OUT_UNITS + q, q % AHEAD
                            if i == 0:
                                pe.wait_ge(g_split, done + min(m * KU + KU, FK))
                            if m == OUT_UNITS - 1:
                                if i == 1:
                                    ada_flush(l * N_MOD + j + ADA_PRE + ADA_IN + f * ADA_OUT, ADA_BANK_OUT)
                                unit_by_tile(u, slot, banks, g_hi, g_lo, m * KU, FK - m * KU)
                            else:
                                unit(u, slot, banks, g_hi, g_lo, m * KU, FK)
                stat(n + 1)

            def mixer(l):
                n = l * 3 + 1
                base = l * LAYER_UNITS + MIX_BASE
                for c in range(2):
                    unit_as_ready(base + c, c, (0, 1), h_hi, h_lo, c * KU, DK, h_round, h_ready, n * DK + c * KU)
                for i in range(1, 4):
                    for c in range(2):
                        unit(base + 2 * i + c, (2 * i + c) % AHEAD, (2 * i, 2 * i + 1), h_hi, h_lo, c * KU, DK)
                pe.wait_ge(glrw_split, l + 1)
                pe.wait_ge(glu_done, l * CK + 2)
                for k in range(DK):
                    nc.tensor.matmul(bank[0][0:2 * RANK, :], glr_w[:, k, :], h_hi[:, k, :], start=k == 0, stop=False)
                    mm = nc.tensor.matmul(bank[0][0:2 * RANK, :], glr_w[:, k, :], h_lo[:, k, :], start=False, stop=k == DK - 1)
                mm.then_inc(glr_done, 1)
                for c in range(2):
                    unit(base + 8 + c, c, (2, 3), h_hi, h_lo, c * KU, DK)
                pe.wait_ge(glr_out, l + 1)
                for t in range(2):
                    mm = nc.tensor.matmul(bank[t][:], up_w[:, t * P:(t + 1) * P], glr[:], start=True, stop=True)
                    mm.then_inc(z_done, 1)
                pe.wait_ge(glu_done, l * CK + CK)
                for c in range(2):
                    unit(base + 10 + c, 2 + c, (4, 5), h_hi, h_lo, c * KU, DK)
                pe.wait_ge(soft, l * 8 + 2)
                vbank = (6, 7, 0, 1)
                for half in range(2):
                    for c in range(2):
                        pe.wait_ge(w_split, base + 12 + 2 * half + c + 1 + AHEAD)
                        slot = 2 * half + c
                        for tb in range(TB):
                            for k in range(KU):
                                kk = c * KU + k
                                mm = three(bank[vbank[tb]][:, half * CU:(half + 1) * CU],
                                           h_hi[:, kk, tb * P:(tb + 1) * P], h_lo[:, kk, tb * P:(tb + 1) * P],
                                           w_hi[:, slot, k, :], w_lo[:, slot, k, :], kk == 0, kk == DK - 1)
                        mm.then_inc(w_used, 1)
                pe.wait_ge(qk_done, l * 10 + 10)
                for t in range(2):
                    for b in range(TB):
                        mm = nc.tensor.transpose(bank[4 + t][:, b * P:(b + 1) * P], k_end[:, t, b * P:(b + 1) * P], ident[:])
                    mm.then_inc(kT_mm, 1)
                for c in range(2):
                    unit(base + 16 + c, c, (2, 3), h_hi, h_lo, c * KU, DK)

                def scores(h):
                    t, s = h // 2, h % 2
                    rows = slice(CHUNK * s, CHUNK * s + CHUNK)
                    fwd, bwd = (6, 7) if s == 0 else (0, 1)
                    for kk, qq, into in ((k_fwd, q_fwd, fwd), (k_bwd, q_bwd, bwd)):
                        for b in range(TB):
                            mm = nc.tensor.matmul(bank[into][:, b * P:(b + 1) * P], kk[rows, t, b * P:(b + 1) * P],
                                                  qq[rows, t, b * P:(b + 1) * P], start=True, stop=True)
                    mm.then_inc(att_mm, 1)

                pe.wait_ge(v_out, l * TB + TB)
                scores(0)
                scores(1)
                pe.wait_ge(kT_out, l * 2 + 2)
                unit(base + 18, 2, (4, 5), h_hi, h_lo, 0, DK)
                pe.wait_ge(att_sel, l * 8 + 4)
                scores(2)
                scores(3)
                unit(base + 19, 3, (4, 5), h_hi, h_lo, KU, DK)
                pe.wait_ge(r_out, l * HEADS + 2)
                pe.wait_ge(pair_sum, l + 1)
                nc.tensor.matmul(bank[2][:], ones[:], tmp[:, 0, :], start=True, stop=False)
                pe.wait_ge(tap_done[2], (l + 1) * TAPS)
                nc.tensor.matmul(bank[2][:], ones[:], conv[:, 2, :], start=False, stop=False)
                pe.wait_ge(pool_tap, (l + 1) * POOL_TAPS)
                nc.tensor.matmul(bank[2][:], ones[:], conv[:, 3, :], start=False, stop=True).then_inc(mean_mm, 1)

                def within(h):
                    for b in range(TB):
                        nc.tensor.matmul(bank[h][:, b * P:(b + 1) * P], v[:, b, h * P:(h + 1) * P],
                                         att[:, h, b * P:(b + 1) * P], start=b == 0, stop=False, skip_group_check=True)

                def from_states(h):
                    t, s = h // 2, h % 2
                    rows = slice(CHUNK * s, CHUNK * s + CHUNK)
                    pe.wait_ge(st, (l * 2 + t + 1) * (NCHUNK - 1))
                    for c in range(1, NCHUNK):
                        mm = nc.tensor.matmul(bank[h][:, c * CHUNK:(c + 1) * CHUNK], state[rows, t, c - 1, :],
                                              q_fwd[rows, t, c * CHUNK:(c + 1) * CHUNK], start=False, stop=c == NCHUNK - 1,
                                              skip_group_check=True)
                    mm.then_inc(o_mm, 1)

                pe.wait_ge(att_sel, l * 8 + 8)
                pe.wait_ge(r_out, l * HEADS + HEADS)
                within(0)
                within(1)
                for t in range(2):
                    for odd in range(2):
                        for s in range(2):
                            for b in range(TB - odd):
                                rows = slice(CHUNK * odd, CHUNK * odd + CHUNK)
                                mm = nc.tensor.matmul(
                                    bank[6 - 2 * t + odd][CHUNK * s:CHUNK * s + CHUNK, b * P:(b + 1) * P],
                                    k_endT[rows, t, b * P + CHUNK * s:b * P + CHUNK * s + CHUNK],
                                    v[rows, b, (2 * t + s) * P:(2 * t + s + 1) * P], start=True, stop=True)
                    mm.then_inc(u_mm, 1)
                pe.wait_ge(sq_sum, l * 2 + 2)
                column_sums(3, 0, glu[:, 0, PAD:PAD + T], True, False)
                pe.wait_ge(c_sq, l * CK + CK)
                column_sums(3, 0, glu[:, 3, PAD:PAD + T], False, True).then_inc(var_mm, 1)
                from_states(0)
                keep_warm(WARM_MIX, 7)
                pe.wait_ge(ln_inv, l + 1)
                along_tokens(3, inv).then_inc(ln_spread, 1)
                keep_warm(WARM_MIX, 7)
                from_states(1)
                keep_warm(WARM_MIX, 7)
                within(2)
                from_states(2)
                keep_warm(WARM_MIX, 7)
                pe.wait_ge(ln_done, l * CK + CK)
                within(3)
                from_states(3)
                out = base + ZIN_UNITS
                pe.wait_ge(y_ready, l * DK + CK)
                unit(out, 0, (4, 5), h_hi, h_lo, 0, DK)

                def conv_half(k):
                    for m in range(2):
                        mm = three(bank[6 + m][:], w_hi[:, 1, k, m * P:(m + 1) * P], w_lo[:, 1, k, m * P:(m + 1) * P],
                                   h_hi[:, k, :], h_lo[:, k, :], k == 0, False)
                    return mm

                pe.wait_ge(o_gated, l * HEADS + 1)
                pe.wait_ge(w_split, out + 1 + 1 + AHEAD)
                for h in range(HEADS):
                    pe.wait_ge(o_sq, l * HEADS + h + 1)
                    mm = column_sums(0, h * TB, o_square(h), h == 0, h == HEADS - 1)
                    if h == HEADS - 1:
                        mm.then_inc(oss_mm, 1)
                    if h % 2:
                        conv_half(h // 2)
                pe.wait_ge(o_inv, l + 1)
                pe.wait_ge(o_gated, l * HEADS + HEADS)
                for h in range(HEADS):
                    along_tokens(h, inv_o[:, h, :]).then_inc(o_spread, 1)
                    if h % 2:
                        mm = conv_half(2 + h // 2)
                mm.then_inc(w_used, 1)
                unit_as_ready(out + 2, 2, (4, 5), h_hi, h_lo, KU, DK, y_round, y_ready, l * DK + CK,
                              ends_pair=True)
                unit_by_tile(out + 3, 3, (6, 7), h_hi, h_lo, KU)
                unit(out + 4, 0, (0, 1), h_hi, h_lo, 0, DK)
                unit_by_tile(out + 5, 1, (0, 1), h_hi, h_lo, KU)
                unit(out + 6, 2, (2, 3), h_hi, h_lo, 0, DK)
                unit_by_tile(out + 7, 3, (2, 3), h_hi, h_lo, KU)
                stat(n + 1)

            pe.wait_ge(const_ready, CONSTS)
            pe.wait_ge(fold_ready, 1)
            for b, acc in enumerate((pre_acc, ada_acc)):
                if b:
                    mean_squares(0)
                    spread_rms(0)
                pe.wait_ge(pre_mac, (b + 1) * DK)
                for n in range(DK):
                    mm = nc.tensor.matmul(bank[ADA_BANK_PRE[b]][:, n:n + 1], acc[:, n * P:(n + 1) * P], ones[:, 0:1],
                                          start=True, stop=True)
                mm.then_inc(ada_sum, 1)
            keep_warm(WARM_PRE)
            with pe.Fori(0, LAYERS) as l:
                ffn(l, 0)
                mixer(l)
                ffn(l, 1)

        @block.scalar
        def _(act):
            def split(grp, q, tiles=KU, used=True):
                grp, slot = grp + q // AHEAD, q % AHEAD
                act.wait_ge(w_loaded[slot], grp * 16 + 16)
                if used:
                    act.wait_ge(w_used, grp * AHEAD + slot - AHEAD + 1)
                nc.scalar.activation(w_hi[:, slot, 0:tiles, :], raw[:, slot, 0:tiles, :], ACT.Copy).then_inc(w_round, 1)

            def root(n):
                act.wait_ge(stat_ready, n + 1)
                nc.scalar.activation(inv[:], bank[STAT][:, 0:TB], ACT.Sqrt, bias=eps[:, 0:1], scale=1.0 / D).then_inc(rms_root, 1)

            def norm(n, shift):
                for k in range(DK):
                    act.wait_ge(xn_ready, n * DK + k + 1)
                    nc.scalar.activation(h_hi[:, k, :], tmp[:, k % 3, :], ACT.Identity,
                                         bias=mod[:, shift, k:k + 1]).then_inc(h_round, 1)

            def square(m, slot, updates, sums):
                act.wait_ge(x_ready, updates + m + 1)
                act.wait_ge(ssq_ready, sums + m)
                nc.scalar.activation(tmp[:, slot, :], x[:, bass.ds(m, 1), :].rearrange("p k t -> p (k t)"),
                                     ACT.Square).then_inc(sq_ready, 1)

            def ffn(l, f):
                n = l * 3 + 2 * f
                grp = l * (LAYER_UNITS // AHEAD) + FFN_BASE[f] // AHEAD
                done = (l * 2 + f) * FK
                norm(n, 6 * f)

                def in_block(b, first):
                    split(grp + b, AHEAD)
                    split(grp + b, AHEAD + 1)
                    if first:
                        act.wait_ge(h_ready, n * DK + DK)
                    else:
                        act.wait_ge(g_split, done + 2 * b)
                    for i in range(2):
                        nc.scalar.activation(tmp[:, i, :], bank[IN_GATE[i]][:], ACT.Silu).then_inc(silu_done, 1)
                    split(grp + b, AHEAD + 2)
                    split(grp + b, AHEAD + 3)
                    for i in range(2):
                        act.wait_ge(g_ready, done + 2 * b + i + 1)
                        nc.scalar.activation(g_hi[:, bass.ds(2 * b + i, 1), :].rearrange("p k t -> p (k t)"), tmp[:, i, :],
                                             ACT.Copy).then_inc(g_round, 1)

                in_block(0, True)
                with act.Fori(0, (BLOCKS - 1) // 2) as j:
                    for i in range(2):
                        in_block(2 * j + 1 + i, False)
                act.wait_ge(g_split, done + FK)
                with act.Fori(0, PAIRS // 2) as j:
                    for i in range(2):
                        def step(m):
                            q = i * OUT_UNITS + m + AHEAD
                            tiles = FK % KU if q % OUT_UNITS == OUT_UNITS - 1 else KU
                            split(grp + BLOCKS + j * (2 * OUT_UNITS // AHEAD), q, tiles)

                        for m in range(OUT_UNITS - 1):
                            step(m)
                        for t in range(2):
                            square(4 * j + 2 * i + t, t, DK + l * 3 * DK + 2 * f * DK, (n + 1) * DK)
                            if t == 0:
                                step(OUT_UNITS - 1)
                root(n + 1)

            def mixer(l):
                n = l * 3 + 1
                grp = l * (LAYER_UNITS // AHEAD) + MIX_BASE // AHEAD

                def step(u):
                    split(grp, u + AHEAD)

                def products(tile, first, last):
                    for j in range(first, last):
                        win, w = glu[:, tile, j:j + T], w_dw[:, tile, j:j + 1]
                        if j == 0:
                            nc.scalar.activation(conv[:, tile, :], win, ACT.Identity, bias=b_dw[:, tile:tile + 1],
                                                 scale=w).then_inc(prod_ready, 1)
                            continue
                        a = j - 1 if tile == 1 else TAPS - 1 + j - HEAD_TAPS
                        if a >= 3:
                            act.wait_ge(pool_tap, l * POOL_TAPS + a - 2)
                        nc.scalar.activation(prod[:, a % 3, :], win, ACT.Copy, scale=w).then_inc(prod_ready, 1)

                norm(n, 3)
                step(0)
                step(1)
                act.wait_ge(mixp_loaded, l * 80 + 80)
                nc.scalar.activation(glr_w[:, :, 0:RANK], glr_raw[:], ACT.Copy).then_inc(glrw_round, 1)
                step(2)
                step(3)
                act.wait_ge(h_ready, n * DK + DK)
                for i in range(2):
                    nc.scalar.activation(tmp[:, i, :], bank[2 + i][:], ACT.Sigmoid).then_inc(sig_done, 1)
                step(4)
                act.wait_ge(built, l * BUILDS + BUILDS)
                act.wait_ge(glu_done, l * CK + 2)
                products(1, 0, 4)
                for u in range(5, 8):
                    step(u)
                    if u < 7:
                        products(1, 4 * (u - 4), 4 * (u - 3))
                for i in range(2):
                    nc.scalar.activation(tmp[:, i, :], bank[6 + i][:], ACT.Sigmoid).then_inc(sig_done, 1)
                products(1, 12, 16)
                act.wait_ge(glr_done, l + 1)
                nc.scalar.activation(glr[:], bank[0][0:2 * RANK, :], ACT.Copy).then_inc(glr_out, 1)
                products(1, 16, 18)
                step(8)
                products(1, 18, 21)
                step(9)
                act.wait_ge(z_done, l * 2 + 2)
                for t in range(2):
                    nc.scalar.activation(k_fwd[:, t, :], bank[t][:], ACT.Identity, bias=b_gate[:, t:t + 1]).then_inc(soft, 1)
                for t in range(2):
                    act.wait_ge(soft, l * 8 + 1 + t)
                    nc.scalar.activation(k_bwd[:, t, :], k_fwd[:, t, :], ACT.Abs).then_inc(soft, 1)
                for t in range(2):
                    act.wait_ge(soft, l * 8 + 3 + t)
                    nc.scalar.activation(k_bwd[:, t, :], k_bwd[:, t, :], ACT.Exp, scale=-1.0).then_inc(soft, 1)
                for t in range(2):
                    act.wait_ge(soft, l * 8 + 5 + t)
                    nc.scalar.activation(k_bwd[:, t, :], k_bwd[:, t, :], ACT.Ln, bias=1.0).then_inc(soft, 1)
                products(1, 21, 25)
                step(10)
                for t in range(2):
                    act.wait_ge(diff, l * 2 + t + 1)
                    ends = bc[:, t, :].rearrange("p (c j) -> p c j", j=CHUNK)[:, :, CHUNK - 1:CHUNK]
                    nc.scalar.activation(k_bwd[:, t, :], bc[:, t, :], ACT.Exp, scale=1.0 / TAU).then_inc(exps, 1)
                    nc.scalar.activation(k_fwd[:, t, :], bc[:, t, :], ACT.Exp, scale=-1.0 / TAU).then_inc(exps, 1)
                    nc.scalar.activation(k_end[:, t, :], k_end[:, t, :], ACT.Exp, scale=1.0 / TAU).then_inc(exps, 1)
                    nc.scalar.activation(end_exp[:, t, :], ends, ACT.Exp, scale=1.0 / TAU).then_inc(exps, 1)
                products(1, 25, 28)
                step(11)
                products(1, 28, 31)
                for u in range(12, 16):
                    step(u)
                    if u < 15:
                        products(3, HEAD_TAPS + 4 * (u - 12), HEAD_TAPS + 4 * (u - 11))
                for tb, b in enumerate((6, 7, 0, 1)):
                    nc.scalar.activation(v[:, tb, :], bank[b][:], ACT.Copy).then_inc(v_out, 1)
                for t in range(2):
                    act.wait_ge(kT_mm, l * 2 + t + 1)
                    nc.scalar.activation(k_endT[:, t, :], bank[4 + t][:], ACT.Copy).then_inc(kT_out, 1)
                products(3, HEAD_TAPS + 12, HEAD_TAPS + 14)
                step(16)
                products(3, HEAD_TAPS + 14, HEAD_TAPS + 17)
                step(17)
                for i in range(2):
                    nc.scalar.activation(r_act[:, i, :], bank[2 + i][:], ACT.Silu).then_inc(r_out, 1)
                products(3, HEAD_TAPS + 17, TAPS)
                step(18)
                step(19)
                for i in range(2):
                    nc.scalar.activation(r_act[:, 2 + i, :], bank[4 + i][:], ACT.Silu).then_inc(r_out, 1)
                for i in range(CK):
                    act.wait_ge(centred, l * CK + i + 1)
                    nc.scalar.activation(glu[:, i, PAD:PAD + T], conv[:, i, :], ACT.Square).then_inc(c_sq, 1)

                def square_head(h):
                    act.wait_ge(o_mm, l * HEADS + h + 1)
                    nc.scalar.activation(o_square(h), bank[h][:], ACT.Square).then_inc(o_sq, 1)

                act.wait_ge(var_mm, l + 1)
                nc.scalar.activation(inv[:], bank[3][:, 0:TB], ACT.Sqrt, bias=eps[:, 0:1],
                                     scale=1.0 / (CK * P)).then_inc(ln_root, 1)
                square_head(0)
                for i in range(CK):
                    act.wait_ge(ln_done, l * CK + i + 1)
                    nc.scalar.activation(conv[:, i, :], conv[:, i, :], ACT.Silu, bias=b_ln[:, i:i + 1],
                                         scale=g_ln[:, i:i + 1]).then_inc(c_act_done, 1)
                for i in range(CK):
                    act.wait_ge(c_act_done, l * CK + i + 1)
                    nc.scalar.activation(h_hi[:, i, :], conv[:, i, :], ACT.Copy).then_inc(y_round, 1)
                for h in range(1, HEADS):
                    square_head(h)
                act.wait_ge(oss_mm, l + 1)
                nc.scalar.activation(inv_o[:].rearrange("p h b -> p (h b)"), bank[0][:, 0:HEADS * TB], ACT.Sqrt,
                                     bias=eps[:, 0:1], scale=1.0 / P).then_inc(o_root, 1)
                step(20)
                for h in range(HEADS):
                    act.wait_ge(o_norm, l * HEADS + h + 1)
                    nc.scalar.activation(h_hi[:, CK + h, :], o_tile(h), ACT.Copy).then_inc(y_round, 1)
                step(21)
                for p_, steps in enumerate(((22,), (23,), (24, 25), (26, 27))):
                    for u in steps[:-1]:
                        step(u)
                    for t in range(2):
                        square(2 * p_ + t, t, DK + l * 3 * DK + DK, (n + 1) * DK)
                    if p_ == PAIRS - 1:
                        root(n + 1)
                    step(steps[-1])

            act.wait_ge(const_ready, CONSTS)
            act.wait_ge(par_loaded, 48)
            nc.scalar.activation(c_act[:], c_act[:], ACT.Silu).then_inc(c_ready, 1)
            act.wait_ge(x_loaded, 16)
            act.wait_ge(w_split, AHEAD)
            for k in range(DK):
                if k >= 1:
                    act.wait_ge(ssq_ready, k)
                nc.scalar.activation(tmp[:, k % 2, :], x[:, k, :], ACT.Square).then_inc(sq_ready, 1)
            root(0)
            for q in range(AHEAD):
                split(0, q, used=False)
            with act.Fori(0, LAYERS) as l:
                ffn(l, 0)
                mixer(l)
                ffn(l, 1)
            for k in range(DK):
                act.wait_ge(xn_ready, 3 * LAYERS * DK + k + 1)
                nc.scalar.activation(x[:, k, :], tmp[:, k % 3, :], ACT.Identity,
                                     bias=mod[:, 0, k:k + 1]).then_inc(final_ready, 1)

        @block.vector
        def _(dve):
            def split(grp, q, tiles=KU):
                grp, slot = grp + q // AHEAD, q % AHEAD
                dve.wait_ge(w_round, grp * AHEAD + slot + 1)
                nc.vector.tensor_tensor(w_lo[:, slot, 0:tiles, :], raw[:, slot, 0:tiles, :],
                                        w_hi[:, slot, 0:tiles, :].bitcast(F32), ALU.subtract).then_inc(w_split, 1)

            def add_slice(blk, k):
                dve.wait_ge(ada_loaded[k % ADA_SLOTS], ((blk - ADA_PRE) * (DK // ADA_SLOTS) + k // ADA_SLOTS) * 16 + 16)
                src = ada_raw[:, k % ADA_SLOTS, :]
                if k == 0:
                    dve.wait_ge(ada_sum, blk)
                    nc.vector.tensor_scalar(ada_acc[:], src, c_act[:, k:k + 1], None, ALU.mult).then_inc(ada_mac, 1)
                else:
                    dve.wait_ge(ada_mac, (blk - ADA_PRE) * DK + k + ADA_SLOTS)
                    nc.vector.scalar_tensor_tensor(ada_acc[:], src, c_act[:, k:k + 1], ada_acc[:], ALU.mult,
                                                   ALU.add).then_inc(ada_mac, 1)

            def fold_ada(blk):
                done = (blk - ADA_PRE) * FOLDS
                dve.wait_ge(ada_mac, (blk - ADA_PRE + 1) * DK + ADA_SLOTS)
                for half in range(2):
                    if half:
                        dve.wait_ge(ada_fold, done + 2)
                    nc.vector.transpose(tmp[:, 2, :], ada_acc[:, half * T:(half + 1) * T]).then_inc(ada_fold, 1)
                    dve.wait_ge(ada_fold, done + 2 * half + 1)
                    nc.vector.tensor_reduce(ada_part[:, half * (T // SQ):(half + 1) * (T // SQ)],
                                            tmp[:, 2, :].rearrange("p (b q) -> p b q", q=SQ), mybir.AxisListType.X,
                                            ALU.add).then_inc(ada_fold, 1)

            def finish_ada(blk, into, at):
                dve.wait_ge(ada_sum, blk + 1)
                nc.vector.tensor_tensor(mod[:, bass.ds(at, 1), :].rearrange("p a k -> p (a k)"), bank[into][:, 0:DK],
                                        b_ada[:, bass.ds(blk, 1), :].rearrange("p a k -> p (a k)"), ALU.add).then_inc(mod_ready, 1)

            def find_gain(n, scale_at, mods):
                dve.wait_ge(mod_ready, mods)
                nc.vector.scalar_tensor_tensor(gain[:], mod[:, scale_at, :], 1.0,
                                               g_norm[:, bass.ds(n, 1), :].rearrange("p a k -> p (a k)"), ALU.add,
                                               ALU.mult).then_inc(gain_ready, 1)

            def inverse(n):
                dve.wait_ge(rms_root, n + 1)
                nc.vector.reciprocal(inv[:], inv[:]).then_inc(rms_step, 1)

            def scale_x(n, k):
                nc.vector.scalar_tensor_tensor(tmp[:, k % 3, :], x[:, k, :], gain[:, k:k + 1], bank[SPREAD][:], ALU.mult,
                                               ALU.mult).then_inc(xn_ready, 1)

            def norm(n, shift):
                dve.wait_ge(gain_ready, n + 1)
                dve.wait_ge(spread, n + 1)
                for k in range(DK + 1):
                    if k < DK:
                        if k >= 3:
                            dve.wait_ge(h_ready, n * DK + k - 2)
                        scale_x(n, k)
                    if k >= 1:
                        dve.wait_ge(h_round, n * DK + k)
                        nc.vector.scalar_tensor_tensor(h_lo[:, k - 1, :], tmp[:, (k - 1) % 3, :], mod[:, shift, k - 1:k],
                                                       h_hi[:, k - 1, :].bitcast(F32), ALU.add, ALU.subtract).then_inc(h_ready, 1)

            def add_squares(slot, at):
                dve.wait_ge(sq_ready, at)
                dve.wait_ge(ssq_ready, at)
                nc.vector.tensor_tensor(ssq[:], ssq[:], tmp[:, 1 - slot, :], ALU.add).then_inc(ssq_ready, 1)

            def clear(what):
                nc.vector.memset(what, 0.0).then_inc(gate_ready, 1)

            def update(m, b, gate_col):
                xm = x[:, bass.ds(m, 1), :].rearrange("p k t -> p (k t)")
                nc.vector.scalar_tensor_tensor(xm, bank[b][:], gate_col, xm, ALU.mult, ALU.add).then_inc(x_ready, 1)

            def ffn(l, f):
                n = l * 3 + 2 * f
                grp = l * (LAYER_UNITS // AHEAD) + FFN_BASE[f] // AHEAD
                done = (l * 2 + f) * FK
                norm(n, 6 * f)

                def ada_work(blk, half, m):
                    if m < 4:
                        for k in ([[0, 1], [2], [3, 4], [5]], [[6, 7], [], [], []])[half][m]:
                            add_slice(blk, k)
                    if half == 1 and m == 0:
                        fold_ada(blk)

                def in_block(b, blk, half):
                    for m in range(4):
                        if m < 3:
                            split(grp + b, AHEAD + m)
                        if blk is not None:
                            ada_work(blk, half, m)
                    split(grp + b, AHEAD + 3)
                    for i in range(2):
                        dve.wait_ge(silu_done, done + 2 * b + i + 1)
                        nc.vector.tensor_tensor(tmp[:, i, :], tmp[:, i, :], bank[IN_UP[i]][:], ALU.mult).then_inc(g_ready, 1)
                    for i in range(2):
                        m = bass.ds(2 * b + i, 1)
                        dve.wait_ge(g_round, done + 2 * b + i + 1)
                        nc.vector.tensor_tensor(g_lo[:, m, :].rearrange("p k t -> p (k t)"), tmp[:, i, :],
                                                g_hi[:, m, :].rearrange("p k t -> p (k t)").bitcast(F32),
                                                ALU.subtract).then_inc(g_split, 1)

                in_block(0, None, 0)
                with dve.Fori(0, (BLOCKS - 1) // 2) as j:
                    blk = l * N_MOD + j + ADA_PRE
                    for i in range(2):
                        in_block(2 * j + 1 + i, blk if f == 0 else None, i)
                    if f == 0:
                        finish_ada(blk, ADA_BANK_IN, j + ADA_PRE)
                dve.wait_ge(mod_ready, l * N_MOD + ADA_PRE + ADA_IN + f * ADA_OUT)
                nc.vector.tensor_scalar(gate[:], mod[:, 2 + 6 * f, :], 0.5, None, ALU.mult).then_inc(gate_ready, 1)
                dve.wait_ge(g_split, done + FK)
                clear(ssq[:])
                clear(tmp[:, 1, :])
                with dve.Fori(0, PAIRS // 2) as j:
                    blk = l * N_MOD + j + ADA_PRE + ADA_IN + f * ADA_OUT
                    for i in range(2):
                        def step(m):
                            q = i * OUT_UNITS + m + AHEAD
                            tiles = FK % KU if q % OUT_UNITS == OUT_UNITS - 1 else KU
                            split(grp + BLOCKS + j * (2 * OUT_UNITS // AHEAD), q, tiles)

                        for m in range(OUT_UNITS - 1):
                            step(m)
                            ada_work(blk, i, m)
                        dve.wait_ge(gate_ready, l * 8 + 5 * f + 3)
                        for t in range(2):
                            m = 4 * j + 2 * i + t
                            if t == 0:
                                dve.wait_ge(even_done, l * 3 * PAIRS + 2 * f * PAIRS + 2 * j + i + 1)
                            else:
                                dve.wait_ge(w_used, l * LAYER_UNITS + FFN_BASE[f] + IN_UNITS + (2 * j + i + 1) * OUT_UNITS)
                            update(m, (OUT_A, OUT_B)[i][t], gate[:, bass.ds(m, 1)])
                            add_squares(t, (n + 1) * DK + m)
                        step(OUT_UNITS - 1)
                    finish_ada(blk, ADA_BANK_OUT, j + (ADA_PRE + ADA_IN if f == 0 else 0))
                find_gain(n + 1, (4, 1)[f], l * N_MOD + ADA_PRE + ADA_IN + (f + 1) * ADA_OUT)
                inverse(n + 1)

            def mixer(l):
                n = l * 3 + 1
                grp = l * (LAYER_UNITS // AHEAD) + MIX_BASE // AHEAD

                def step(u):
                    split(grp, u + AHEAD)

                def conv_taps(tile, first, last):
                    for j in range(first, last):
                        win, w = glu[:, tile, j:j + T], w_dw[:, tile, j:j + 1]
                        if j == 0:
                            ins = nc.vector.tensor_scalar(conv[:, tile, :], win, w, b_dw[:, tile:tile + 1], ALU.mult, ALU.add)
                        else:
                            dve.wait_ge(tap_done[tile], l * tap_total[tile] + j)
                            ins = nc.vector.scalar_tensor_tensor(conv[:, tile, :], win, w, conv[:, tile, :], ALU.mult, ALU.add)
                        ins.then_inc(tap_done[tile], 1)

                norm(n, 3)
                step(0)
                step(1)
                dve.wait_ge(glrw_round, l + 1)
                nc.vector.tensor_tensor(glr_w[:, :, RANK:2 * RANK], glr_raw[:], glr_w[:, :, 0:RANK].bitcast(F32), ALU.subtract).then_inc(glrw_split, 1)
                step(2)
                step(3)
                for i in range(2):
                    dve.wait_ge(sig_done, l * CK + i + 1)
                    nc.vector.tensor_tensor(glu[:, i, PAD:PAD + T], tmp[:, i, :], bank[i][:], ALU.mult).then_inc(glu_done, 1)
                dve.wait_ge(built, l * BUILDS + BUILDS)
                dve.wait_ge(glu_done, l * CK + 2)
                for u in range(4, 7):
                    step(u)
                    conv_taps(0, 5 * (u - 4), 5 * (u - 3))
                step(7)
                for i in range(2):
                    dve.wait_ge(sig_done, l * CK + 2 + i + 1)
                    nc.vector.tensor_tensor(glu[:, 2 + i, PAD:PAD + T], tmp[:, i, :], bank[4 + i][:], ALU.mult).then_inc(glu_done, 1)
                conv_taps(0, 15, 20)
                conv_taps(3, 0, 5)
                step(8)
                conv_taps(0, 20, 23)
                conv_taps(3, 5, 7)
                step(9)
                conv_taps(0, 23, 30)
                for t in range(2):
                    dve.wait_ge(soft, l * 8 + 7 + t)
                    nc.vector.scalar_tensor_tensor(q_fwd[:, t, :], k_fwd[:, t, :], 0.0, k_bwd[:, t, :], ALU.min,
                                                   ALU.subtract).then_inc(logsig, 1)
                for t in range(2):
                    dve.wait_ge(logsig, l * 2 + t + 1)
                    nc.vector.tensor_tensor_scan(bc[:, t, :], restart[:], q_fwd[:, t, :], 0.0, ALU.mult, ALU.add).then_inc(scanned, 1)
                for t in range(2):
                    dve.wait_ge(scanned, l * 2 + t + 1)
                    b3 = bc[:, t, :].rearrange("p (c j) -> p c j", j=CHUNK)
                    nc.vector.tensor_tensor(k_end[:, t, :].rearrange("p (c j) -> p c j", j=CHUNK),
                                            b3[:, :, CHUNK - 1:CHUNK].to_broadcast([P, NCHUNK, CHUNK]), b3,
                                            ALU.subtract).then_inc(diff, 1)
                step(10)
                conv_taps(0, 30, TAPS)
                conv_taps(3, 7, HEAD_TAPS)
                dve.wait_ge(exps, l * 8 + 8)
                for t in range(2):
                    for out, ex in ((q_fwd, k_bwd), (q_bwd, k_fwd)):
                        nc.vector.scalar_tensor_tensor(out[:, t, :], bank[2 + t][:], CHUNK ** -0.5, ex[:, t, :], ALU.mult,
                                                       ALU.mult).then_inc(qk_done, 1)
                step(11)
                for t in range(2):
                    for ex in (k_bwd, k_fwd, k_end):
                        nc.vector.tensor_tensor(ex[:, t, :], ex[:, t, :], bank[4 + t][:], ALU.mult).then_inc(qk_done, 1)
                conv_taps(2, 0, 4)
                for u in range(12, 16):
                    step(u)
                    conv_taps(2, 4 + 5 * (u - 12), 4 + 5 * (u - 11))
                step(16)
                dve.wait_ge(tap_done[0], (l + 1) * TAPS)
                dve.wait_ge(pool_tap, l * POOL_TAPS + TAPS - 1)
                nc.vector.tensor_tensor(tmp[:, 0, :], conv[:, 0, :], conv[:, 1, :], ALU.add).then_inc(pair_sum, 1)

                def select(mask, heads, banks):
                    for h, b in zip(heads, banks):
                        where = mask[:].bitcast(U32).rearrange("p (o i) -> p o i", o=1).to_broadcast([P, TB, P])
                        nc.vector.copy_predicated(att[:, h, :].rearrange("p (b i) -> p b i", i=P), where,
                                                  bank[b][:].rearrange("p (b i) -> p b i", i=P)).then_inc(att_sel, 1)

                def centre(i):
                    nc.vector.scalar_tensor_tensor(conv[:, i, :], bank[2][:], -1.0 / (CK * P), conv[:, i, :], ALU.mult,
                                                   ALU.add).then_inc(centred, 1)

                def states(t):
                    dve.wait_ge(u_mm, l * 2 + t + 1)
                    for c in range(NCHUNK - 1):
                        u = bank[6 - 2 * t + c % 2][:, (c // 2) * P:(c // 2 + 1) * P]
                        if c == 0:
                            ins = nc.vector.tensor_copy(state[:, t, 0, :], u)
                        else:
                            dve.wait_ge(st, (l * 2 + t) * (NCHUNK - 1) + c)
                            ins = nc.vector.scalar_tensor_tensor(state[:, t, c, :], state[:, t, c - 1, :], end_exp[:, t, c:c + 1],
                                                                 u, ALU.mult, ALU.add)
                        ins.then_inc(st, 1)

                dve.wait_ge(att_mm, l * HEADS + 2)
                conv_taps(2, 24, 25)
                select(mask_f, (0, 1), (6, 0))
                dve.wait_ge(att_sel, l * 8 + 2)
                conv_taps(2, 25, 26)
                select(mask_b, (0, 1), (7, 1))
                step(17)
                conv_taps(2, 26, TAPS)
                step(18)
                dve.wait_ge(att_mm, l * HEADS + HEADS)
                clear(ssq[:])
                select(mask_f, (2, 3), (6, 0))
                dve.wait_ge(att_sel, l * 8 + 6)
                clear(tmp[:, 1, :])
                select(mask_b, (2, 3), (7, 1))
                step(19)
                dve.wait_ge(mean_mm, l + 1)
                for i in range(CK):
                    centre(i)
                dve.wait_ge(c_sq, l * CK + 2)
                first = glu[:, 0, PAD:PAD + T]
                nc.vector.tensor_tensor(first, first, glu[:, 1, PAD:PAD + T], ALU.add).then_inc(sq_sum, 1)
                dve.wait_ge(c_sq, l * CK + 3)
                dve.wait_ge(sq_sum, l * 2 + 1)
                nc.vector.tensor_tensor(first, first, glu[:, 2, PAD:PAD + T], ALU.add).then_inc(sq_sum, 1)
                states(0)
                dve.wait_ge(ln_root, l + 1)
                nc.vector.reciprocal(inv[:], inv[:]).then_inc(ln_inv, 1)
                states(1)
                dve.wait_ge(ln_spread, l + 1)
                for i in range(CK):
                    nc.vector.tensor_tensor(conv[:, i, :], conv[:, i, :], bank[3][:], ALU.mult).then_inc(ln_done, 1)
                for i in range(CK):
                    dve.wait_ge(y_round, l * DK + i + 1)
                    nc.vector.tensor_tensor(h_lo[:, i, :], conv[:, i, :], h_hi[:, i, :].bitcast(F32), ALU.subtract).then_inc(y_ready, 1)
                for h in range(HEADS):
                    dve.wait_ge(o_sq, l * HEADS + h + 1)
                    nc.vector.scalar_tensor_tensor(o_tile(h), bank[h][:], g_gla[:, h:h + 1], r_act[:, h, :], ALU.mult,
                                                   ALU.mult).then_inc(o_gated, 1)
                dve.wait_ge(o_root, l + 1)
                nc.vector.reciprocal(inv_o[:], inv_o[:]).then_inc(o_inv, 1)
                step(20)
                for h in range(HEADS + 1):
                    if h < HEADS:
                        dve.wait_ge(o_spread, l * HEADS + h + 1)
                        nc.vector.tensor_tensor(o_tile(h), o_tile(h), bank[h][:], ALU.mult).then_inc(o_norm, 1)
                    if h:
                        dve.wait_ge(y_round, l * DK + CK + h)
                        nc.vector.tensor_tensor(h_lo[:, CK + h - 1, :], o_tile(h - 1), h_hi[:, CK + h - 1, :].bitcast(F32),
                                                ALU.subtract).then_inc(y_ready, 1)
                step(21)
                dve.wait_ge(gate_ready, l * 8 + 5)
                for p_, steps in enumerate(((22,), (23,), (24, 25), (26, 27))):
                    for u in steps[:-1]:
                        step(u)
                    for t in range(2):
                        m = 2 * p_ + t
                        if t == 0:
                            dve.wait_ge(even_done, l * 3 * PAIRS + PAIRS + p_ + 1)
                        else:
                            dve.wait_ge(w_used, l * LAYER_UNITS + MIX_BASE + steps[-1] + 1)
                        update(m, (4, 6, 0, 2)[p_] + t, mod[:, 5, m:m + 1])
                        add_squares(t, (n + 1) * DK + m)
                    if p_ == PAIRS - 1:
                        find_gain(n + 1, 7, l * N_MOD + ADA_PRE + ADA_IN + ADA_OUT)
                        inverse(n + 1)
                    step(steps[-1])

            dve.wait_ge(const_ready, CONSTS)
            nc.vector.tensor_reduce(fold[:], ident[:].rearrange("p (q i) -> p i q", i=SQ), mybir.AxisListType.X,
                                    ALU.add).then_inc(fold_ready, 1)
            nc.vector.memset(ssq[:], 0.0).then_inc(ada_mac, ADA_SLOTS)
            nc.vector.memset(gain[:, 0:1], 0.0).then_inc(x_ready, DK)
            nc.vector.memset(tmp[:, 1, :], 0.0).then_inc(w_split, AHEAD)
            dve.wait_ge(ada_mac, ADA_SLOTS)
            dve.wait_ge(w_split, AHEAD)
            dve.wait_ge(c_ready, 1)
            for b, acc in enumerate((pre_acc, ada_acc)):
                for k in range(DK):
                    dve.wait_ge(pre_loaded[b * DK + k], 16)
                    if k == 0:
                        nc.vector.tensor_scalar(acc[:], pre[:, b, k, :], c_act[:, k:k + 1], None, ALU.mult).then_inc(pre_mac, 1)
                    else:
                        dve.wait_ge(pre_mac, b * DK + k)
                        nc.vector.scalar_tensor_tensor(acc[:], pre[:, b, k, :], c_act[:, k:k + 1], acc[:], ALU.mult,
                                                       ALU.add).then_inc(pre_mac, 1)
                    if b == 0:
                        if k:
                            dve.wait_ge(sq_ready, k)
                            dve.wait_ge(ssq_ready, k)
                        nc.vector.tensor_tensor(ssq[:], ssq[:], tmp[:, 1 - k % 2, :], ALU.add).then_inc(ssq_ready, 1)
                    elif k == DK - 3:
                        inverse(0)
            for q in range(AHEAD):
                if q == 1:
                    finish_ada(0, ADA_BANK_PRE[0], 0)
                split(0, q)
            finish_ada(1, ADA_BANK_PRE[1], 1)
            find_gain(0, 1, ADA_PRE)
            with dve.Fori(0, LAYERS) as l:
                ffn(l, 0)
                mixer(l)
                ffn(l, 1)
            dve.wait_ge(gain_ready, 3 * LAYERS + 1)
            dve.wait_ge(spread, 3 * LAYERS + 1)
            for k in range(DK):
                if k >= 3:
                    dve.wait_ge(final_ready, k - 2)
                scale_x(3 * LAYERS, k)


def kernel(**inputs):
    import numpy as np
    import concourse.bacc as bacc
    from concourse import mybir as mb
    from concourse.bass_utils import run_bass_kernel_spmd

    a = {n: np.asarray(v) for n, v in inputs.items()}
    L = LAYERS

    def columns(z):
        z = z.reshape(*z.shape[:-1], -1, P)
        return np.moveaxis(z, -1, 0)

    laid = {
        "xT": a["x"][0].T,
        "cT": columns(a["c"][0]),
        "w_ada": np.concatenate([*a["w_ada"], a["w_ada_final"]], axis=1),
        "b_adaT": columns(np.concatenate([a["b_ada"].reshape(-1), a["b_ada_final"]]).reshape(-1, D)),
        "g_normT": columns(np.stack([z for l in range(L) for z in (a["g_norm_ffn1"][l], a["g_norm_mix"][l], a["g_norm_ffn2"][l])]
                                    + [a["g_norm_final"]])),
        "w_ffn1_in": a["w_ffn1_in"], "w_ffn1_out": a["w_ffn1_out"], "w_in": a["w_in"],
        "w_glr": np.moveaxis(a["w_in"][:, :, GLR_COL:].reshape(L * DK, P, RANK), 1, 0),
        "w_ffn2_in": a["w_ffn2_in"], "w_ffn2_out": a["w_ffn2_out"], "w_out": a["w_out"],
        "w_dwT": np.moveaxis(columns(a["w_dw"]), 2, 3),
        "mix_colsT": np.concatenate([columns(a[n]) for n in ("b_dw", "g_conv_ln", "b_conv_ln", "b_gate")]
                                    + [columns(a["g_gla_norm"].reshape(L, -1))], axis=2),
        "w_gate_up": np.moveaxis(a["w_gate_up"], 1, 0),
    }
    nc = bacc.Bacc("TRN2", target_bir_lowering=False, num_devices=1)
    arrays, args = {}, []
    for name, z in laid.items():
        z = np.ascontiguousarray(z)
        arrays[f"in_{name}"] = z
        args.append(nc.dram_tensor(f"in_{name}", z.shape, mb.dt.from_np(z.dtype), kind="ExternalInput").ap())
    args.append(nc.dram_tensor("out_T", (D, T), F32, kind="ExternalOutput").ap())
    trunk(nc, *args)
    r = run_bass_kernel_spmd(nc, [arrays], core_ids=[0])
    return np.ascontiguousarray(r.results[0]["out_T"].T)[None]
```
